# Optimizing a Trainium2 kernel written in Bass

```python
import math
import jax, jax.numpy as jnp
from jax import lax
import numpy as np

D_MODEL = 1024
BATCH = 1
SEQ = 256
DEPTH = 1

CHUNK = 64
EPS = 1e-6
PLE_DIM = 256
POOL_W = D_MODEL
POOL_WINDOWS = (2, 4, 8, 16)
POOL_GROUPS = len(POOL_WINDOWS)
POOL_GROUP_W = POOL_W // POOL_GROUPS
RET_HEADS = 4
RET_QK_HEAD = D_MODEL // RET_HEADS
RET_V_HEAD = 2 * RET_QK_HEAD
RET_QK_W = RET_HEADS * RET_QK_HEAD
RET_V_W = RET_HEADS * RET_V_HEAD
ROPE_BASE = 10000.0
IN_SPLITS = (POOL_W, RET_QK_W, RET_QK_W, RET_V_W, RET_V_W, D_MODEL, D_MODEL)
IN_W = sum(IN_SPLITS)
N_EXPERTS = 32
TOP_K = 4
D_FF = D_MODEL
SWIGLU_ALPHA = 1.702
SWIGLU_LIMIT = 7.0
MOE_BLOCK = 256

kernel_name = "hybrid_pool_retention_moe_block"

def _rmsnorm(x, g):
    x32 = x.astype(jnp.float32)
    y = x32 * lax.rsqrt(jnp.mean(x32 * x32, axis=-1, keepdims=True) + EPS)
    return (y * g.astype(jnp.float32)).astype(x.dtype)

def _multiscale_pool(u, w_pool, scale):
    b, s, _ = u.shape
    u32 = u.astype(jnp.float32).reshape(b, s, POOL_GROUPS, POOL_GROUP_W)
    cs = jnp.cumsum(u32, axis=1)
    t = jnp.arange(s, dtype=jnp.float32)
    outs = []
    for g, w in enumerate(POOL_WINDOWS):
        cg = cs[:, :, g]
        lag = jnp.pad(cg, ((0, 0), (w, 0), (0, 0)))[:, :s]
        count = jnp.minimum(t + 1.0, float(w))[None, :, None]
        pooled = (cg - lag) / count - u32[:, :, g]
        outs.append(jnp.einsum('bsc,cd->bsd', pooled.astype(u.dtype), w_pool[g]))
    return jnp.concatenate(outs, axis=-1) * scale

def _rotary(x, pos):
    half = x.shape[-1] // 2
    inv = ROPE_BASE ** (-jnp.linspace(0.0, 1.0, half, dtype=jnp.float32))
    ang = pos[:, None] * inv[None, :]
    cos = jnp.cos(ang)[None, :, None, :]
    sin = jnp.sin(ang)[None, :, None, :]
    x1, x2 = x[..., :half], x[..., half:]
    return jnp.concatenate([x1 * cos - x2 * sin, x2 * cos + x1 * sin], axis=-1)

def _retention(q, k, v):
    b, s, h, dk = q.shape
    dv = v.shape[-1]
    nc = s // CHUNK
    log_g = jnp.log(1.0 - 2.0 ** (-5.0 - jnp.arange(h, dtype=jnp.float32)))
    idx = jnp.arange(CHUNK, dtype=jnp.float32)
    intra = jnp.exp(log_g[:, None, None] * jnp.abs(idx[:, None] - idx[None, :]))
    q_dec = jnp.exp(log_g[:, None] * (idx + 1.0))[:, :, None]
    k_dec = jnp.exp(log_g[:, None] * (CHUNK - 1.0 - idx))[:, :, None]
    c_dec = jnp.exp(log_g * CHUNK)[:, None, None]

    def to_chunks(t):
        return t.reshape(b, nc, CHUNK, h, t.shape[-1]).transpose(1, 0, 3, 2, 4)

    def step(state, inp):
        qc, kc, vc = inp
        scores = jnp.einsum('bhid,bhjd->bhij', qc, kc) * intra
        o = (jnp.einsum('bhij,bhjv->bhiv', scores, vc)
             + jnp.einsum('bhid,bhdv->bhiv', qc * q_dec, state))
        state = state * c_dec + jnp.einsum('bhjd,bhjv->bhdv', kc * k_dec, vc)
        return state, o

    state0 = jnp.zeros((b, h, dk, dv), jnp.float32)
    _, o = lax.scan(step, state0, (to_chunks(q), to_chunks(k), to_chunks(v)))
    return o.transpose(1, 0, 3, 2, 4).reshape(b, s, h, dv)

def _moe(h2, w_router, b_router, w_gate_up, b_gate_up, w_down, b_down):
    t, d = h2.shape
    logits = h2.astype(jnp.float32) @ w_router.astype(jnp.float32) + b_router.astype(jnp.float32)
    top_v, top_i = lax.top_k(logits, TOP_K)
    gates = jax.nn.softmax(top_v, axis=-1)
    n_assign = t * TOP_K
    flat_e = top_i.reshape(-1)
    flat_tok = jnp.repeat(jnp.arange(t, dtype=jnp.int32), TOP_K)
    flat_w = gates.reshape(-1)
    order = jnp.argsort(flat_e)
    sorted_e = flat_e[order]
    counts = jnp.bincount(flat_e, length=N_EXPERTS)
    padded = ((counts + MOE_BLOCK - 1) // MOE_BLOCK) * MOE_BLOCK
    ends_pad = jnp.cumsum(padded)
    starts_pad = ends_pad - padded
    starts = jnp.cumsum(counts) - counts
    rank = jnp.arange(n_assign, dtype=jnp.int32) - starts[sorted_e]
    dest = starts_pad[sorted_e] + rank
    n_buf = n_assign + N_EXPERTS * MOE_BLOCK
    n_blocks = n_buf // MOE_BLOCK
    tok_buf = jnp.full((n_buf,), t, jnp.int32).at[dest].set(flat_tok[order])
    w_buf = jnp.zeros((n_buf,), jnp.float32).at[dest].set(flat_w[order])
    block_e = jnp.minimum(
        jnp.searchsorted(ends_pad, jnp.arange(n_blocks, dtype=ends_pad.dtype) * MOE_BLOCK, side='right'),
        N_EXPERTS - 1)
    h_pad = jnp.concatenate([h2, jnp.zeros((1, d), h2.dtype)], axis=0)

    def expert_block(args):
        tok, wts, e = args
        xb = h_pad[tok]
        gu = xb @ w_gate_up[e] + b_gate_up[e]
        glu, lin = gu[:, :D_FF], gu[:, D_FF:]
        glu = jnp.minimum(glu, SWIGLU_LIMIT)
        lin = jnp.clip(lin, -SWIGLU_LIMIT, SWIGLU_LIMIT)
        act = glu * jax.nn.sigmoid(SWIGLU_ALPHA * glu) * (lin + 1.0)
        y = act @ w_down[e] + b_down[e]
        return y.astype(jnp.float32) * wts[:, None]

    y_buf = lax.map(expert_block, (tok_buf.reshape(n_blocks, MOE_BLOCK),
                                   w_buf.reshape(n_blocks, MOE_BLOCK), block_e))
    out = jax.ops.segment_sum(y_buf.reshape(n_buf, d), tok_buf, num_segments=t + 1)[:t]
    return out.astype(h2.dtype)

def setup_inputs(seed: int = 0) -> dict:
    key = jax.random.key(seed)
    ks = jax.random.split(key, 20)
    f32 = jnp.float32

    def nrm(k, shape, fan_in):
        return jax.random.normal(k, shape, f32) * (fan_in ** -0.5)

    def gain(k, shape):
        return 1.0 + 0.05 * jax.random.normal(k, shape, f32)

    return {
        "x": jax.random.normal(ks[0], (BATCH, SEQ, D_MODEL), f32),
        "p": jax.random.normal(ks[1], (DEPTH, BATCH, SEQ, PLE_DIM), f32),
        "g_mix": gain(ks[2], (DEPTH, D_MODEL)),
        "w_in": nrm(ks[3], (DEPTH, D_MODEL, IN_W), D_MODEL),
        "w_pool": nrm(ks[4], (DEPTH, POOL_GROUPS, POOL_GROUP_W, POOL_GROUP_W), POOL_GROUP_W),
        "pool_scale": gain(ks[5], (DEPTH, POOL_W)),
        "w_ret_o": nrm(ks[6], (DEPTH, RET_V_W, D_MODEL), RET_V_W),
        "w_out": nrm(ks[7], (DEPTH, D_MODEL, D_MODEL), D_MODEL),
        "g_ffn": gain(ks[8], (DEPTH, D_MODEL)),
        "w_router": nrm(ks[9], (DEPTH, D_MODEL, N_EXPERTS), D_MODEL),
        "b_router": 0.01 * jax.random.normal(ks[10], (DEPTH, N_EXPERTS), f32),
        "w_gate_up": nrm(ks[11], (DEPTH, N_EXPERTS, D_MODEL, 2 * D_FF), D_MODEL),
        "b_gate_up": 0.02 * jax.random.normal(ks[12], (DEPTH, N_EXPERTS, 2 * D_FF), f32),
        "w_down": nrm(ks[13], (DEPTH, N_EXPERTS, D_FF, D_MODEL), D_FF),
        "b_down": 0.02 * jax.random.normal(ks[14], (DEPTH, N_EXPERTS, D_MODEL), f32),
        "g_ple": gain(ks[15], (DEPTH, D_MODEL)),
        "w_ple_gate": nrm(ks[16], (DEPTH, D_MODEL, D_MODEL), D_MODEL),
        "w_ple": nrm(ks[17], (DEPTH, PLE_DIM, D_MODEL), PLE_DIM),
        "g_final": gain(ks[18], (D_MODEL,)),
    }

def reference(x, p, g_mix, w_in, w_pool, pool_scale, w_ret_o, w_out,
              g_ffn, w_router, b_router, w_gate_up, b_gate_up, w_down, b_down,
              g_ple, w_ple_gate, w_ple, g_final):
    b, s, d = x.shape
    pos = jnp.arange(s, dtype=jnp.float32)
    split_at = list(np.cumsum(IN_SPLITS)[:-1])
    for i in range(DEPTH):
        h = _rmsnorm(x, g_mix[i])
        proj = h @ w_in[i]
        u_pool, q, k, v, g_ret, gate_a, gate_b = jnp.split(proj, split_at, axis=-1)
        y_pool = _multiscale_pool(u_pool, w_pool[i], pool_scale[i])
        q = _rotary(q.astype(jnp.float32).reshape(b, s, RET_HEADS, RET_QK_HEAD), pos)
        k = _rotary(k.astype(jnp.float32).reshape(b, s, RET_HEADS, RET_QK_HEAD), pos) * (RET_QK_HEAD ** -0.5)
        v = v.astype(jnp.float32).reshape(b, s, RET_HEADS, RET_V_HEAD)
        o = _retention(q, k, v)
        o = o * lax.rsqrt(jnp.mean(o * o, axis=-1, keepdims=True) + EPS)
        o = o.reshape(b, s, RET_V_W) * jax.nn.silu(g_ret.astype(jnp.float32))
        y_ret = o.astype(x.dtype) @ w_ret_o[i]
        merged = jax.nn.sigmoid(gate_a) * y_pool + jax.nn.sigmoid(gate_b) * y_ret
        x = x + merged @ w_out[i]
        h2 = _rmsnorm(x, g_ffn[i]).reshape(b * s, d)
        x = x + _moe(h2, w_router[i], b_router[i], w_gate_up[i], b_gate_up[i],
                     w_down[i], b_down[i]).reshape(b, s, d)
        u = _rmsnorm(x, g_ple[i])
        x = x + jax.nn.sigmoid(u @ w_ple_gate[i]) * (p[i] @ w_ple[i])
    return _rmsnorm(x, g_final)


_drawn_inputs = setup_inputs


def setup_inputs(seed=0):
    import zlib

    import numpy as np

    out = dict(_drawn_inputs(seed))
    spreads = {}
    factors = {'b_gate_up': 6.136, 'b_down': 7.105, 'g_ple': 7.386}
    for name, (base, spread) in spreads.items():
        noise = np.random.default_rng([zlib.crc32(name.encode()), seed]).standard_normal(out[name].shape)
        drawn = base * np.exp(spread * noise) if base else spread * noise
        out[name] = __import__('jax').numpy.asarray(drawn.astype(out[name].dtype))
    for name, factor in factors.items():
        out[name] = (out[name] * factor).astype(out[name].dtype)
    return out
```

```python
from contextlib import ExitStack

import numpy as np

import concourse.bass as bass
from concourse import mybir

F32 = mybir.dt.float32
BF16 = mybir.dt.bfloat16
I32 = mybir.dt.int32
U32 = mybir.dt.uint32
ALU = mybir.AluOpType
ACT = mybir.ActivationFunctionType
AX_X = mybir.AxisListType.X

P = 128
D = 1024
S = 256
KT = D // P
TT = S // P
PLE = 256
HEADS = 4
DV = 2 * D // HEADS
NE = 32
TOPK = 4
FF = 1024
CHUNK = 64
EPS = 1e-6
ALPHA = 1.702
LIMIT = 7.0
WINDOWS = (2, 4, 8, 16)
PAD = max(WINDOWS)
HALF = 512
CAP = 64
MAX_BLOCKS = S // CAP
SLOTS = 6
SLOT = 4096

COL = {"pool": 0, "q": D, "k": 2 * D, "v": 3 * D, "gr": 5 * D, "ga": 7 * D, "gb": 8 * D}

CHUNKS = ([("q", 0), ("k", 0), ("q", 1), ("k", 1)] + [("v", h) for h in range(HEADS)] + [("wpool", 0)]
          + [(k, j) for k in ("pool", "ga", "gb") for j in range(2)] + [("gr", j) for j in range(4)]
          + [("ro", j) for j in range(4)] + [("wo", j) for j in range(2)])
N1 = len(CHUNKS)
TILES = []
for _kind, _j in CHUNKS:
    if _kind == "ro":
        TILES.append((_kind, _j))
    elif _kind != "wpool":
        TILES += [(_kind, 2 * _j), (_kind, 2 * _j + 1)]
TILE = {x: n for n, x in enumerate(TILES)}

JOBS = [("vec", 0)] + [("xT", j) for j in range(4)] + [("pT", 0)]
for _h in range(HEADS):
    JOBS.append(("scores", _h))
for _h in range(HEADS):
    JOBS += [("o", 2 * _h), ("o", 2 * _h + 1), ("ss", _h)]
JOBS += [("ypool", g) for g in range(4)]
JOBS += [("hT", j) for j in range(4)] + [("logits", 0), ("logitsT", 0), ("gT", 0), ("rank", 0)]
JOB = {x: n for n, x in enumerate(JOBS)}


def job_done(kind, j=0):
    return JOB[kind, j] + 1


def tile_done(kind, j=0):
    return TILE[kind, j] + 1


def build_kernel(nc, x, p, g_mix, w_in, w_pool, pool_scale, w_ret_o, w_out, g_ffn, w_router, b_router,
                 w_gate_up, b_gate_up, w_down, b_down, g_ple, w_ple_gate, w_ple, g_final,
                 c_rot, c_decay, c_count, out):
    x_v = x[0].rearrange("(t p) d -> p t d", p=P)
    out_v = out[0].rearrange("(t p) d -> p t d", p=P)
    p_v = p[0, 0].rearrange("(t p) d -> p t d", p=P)
    w_in_v = w_in[0].rearrange("(k p) n -> p k n", p=P)
    w_pool_v = w_pool[0].rearrange("g (c p) d -> p g c d", p=P)
    w_ro_v = w_ret_o[0].rearrange("(k p) n -> p k n", p=P)
    w_out_v = w_out[0].rearrange("(k p) n -> p k n", p=P)
    w_pg_v = w_ple_gate[0].rearrange("(k p) n -> p k n", p=P)
    w_ple_v = w_ple[0].rearrange("(k p) n -> p k n", p=P)

    with ExitStack() as ctx:
        def sb(name, shape, dt=F32):
            return ctx.enter_context(nc.sbuf_tensor(name, shape, dt))

        def sem(name):
            return ctx.enter_context(nc.semaphore(name))

        ring = sb("ring", [P, SLOTS, SLOT])
        xs = sb("xs", [P, TT, D])
        hT = sb("hT", [P, KT, S])
        m = sb("m", [P, KT, S])
        sigB = sb("sigB", [P, KT, S])
        oT = sb("oT", [P, 16, S])
        arena = sb("arena", [P, 9312])
        bias_parts = sb("bias_parts", [96, 2 * FF], BF16)
        wrt = sb("wrt", [P, KT, NE])
        pT = sb("pT", [P, 2, S])
        ident = sb("ident", [P, P])
        ones = sb("ones", [P, P])
        onesb = sb("onesb", [P, P], BF16)
        before = sb("before", [P, P], BF16)
        pick = sb("pick", [96, NE])
        slots_io = sb("slots_io", [P, MAX_BLOCKS + 1, 2, CAP])
        exp_io = sb("exp_io", [P, NE])
        steps64 = sb("steps64", [1, MAX_BLOCKS])
        eps_t = sb("eps_t", [P, 1])
        vrow = sb("vrow", [32, P])
        vec = sb("vec", [P, 4, KT])
        brt = sb("brt", [NE, 1])
        stat = sb("stat", [P, 8, TT])
        LT = sb("LT", [NE, S])
        L = sb("L", [P, TT, NE])
        top = sb("top", [P, TT, 8])
        topi = sb("topi", [P, TT, 8], U32)
        topf = sb("topf", [P, TT, 8])
        Msel = sb("Msel", [P, TT, NE])
        Mb = sb("Mb", [P, TT, NE], BF16)
        Eg = sb("Eg", [P, TT, NE])
        G = sb("G", [P, TT, NE])
        GT = sb("GT", [NE, S])
        pos = sb("pos", [P, TT, NE])
        nit = sb("nit", [1, 8])
        nitems = sb("nitems", [1, 1], I32)

        cut = [0]

        def part(words):
            cut[0] += words
            assert cut[0] <= 9312
            return arena[:, cut[0] - words:cut[0]]

        v = part(2048).rearrange("p (b t n) -> p b t n", b=2, t=TT)
        sT = part(1536).rearrange("p (h n) -> p h n", h=HEADS)
        dec = part(1536).rearrange("p (h n) -> p h n", h=HEADS)
        rot = part(512).rearrange("p (a t) -> p a t", a=2)
        osq = part(1024).rearrange("p (b a t) -> p b a t", b=2, a=2)
        rr = part(256)
        start_rot = cut[0]
        qr = part(1024).rearrange("p (b a t) -> p b a t", b=2, a=2)
        kr = part(1024).rearrange("p (b a t) -> p b a t", b=2, a=2)
        cut[0] = start_rot
        pu = part(2 * (PAD + S)).rearrange("p (a t) -> p a t", a=2)
        pa = part(2 * (PAD + S)).rearrange("p (a t) -> p a t", a=2)
        pb = part(2 * (PAD + S)).rearrange("p (a t) -> p a t", a=2)
        cut[0] = start_rot + 2048
        recip_count = sb("recip_count", [P, 4, S])
        cut[0] = 0
        parts = part(3072).bitcast(BF16).rearrange("p (c t d) -> p c t d", c=3, t=TT)
        resid = part(2048).rearrange("p (t d) -> p t d", t=TT)
        XT = part(512).rearrange("p (k s) -> p k s", k=KT)
        Cg = part(256).rearrange("p (t s) -> p t s", t=TT)
        CT = part(256).rearrange("p (t s) -> p t s", t=TT)
        hot = part(64).bitcast(BF16).rearrange("p (t s) -> p t s", t=TT)
        bsel = part(32).bitcast(BF16)
        g7, gs, l7, act = part(512), part(512), part(512), part(512)
        aT = part(512).rearrange("p (j h s) -> p j h s", j=4, h=2)
        y = part(512)
        tmp = sb("tmp", [P, 2, 512])
        bgu = sigB[0:96].rearrange("p k t -> p (k t)")
        prow = m[:, 0:2, :]
        xn = oT[:, 0:8, :].rearrange("p (t c) s -> p t (c s)", t=TT)
        junk = oT[:, 8:12, :].rearrange("p c s -> p (c s)")
        bdown = sigB[0:NE, 0:4, :].rearrange("p k t -> p (k t)")
        gfin = sigB[:, 4:8, :].rearrange("p k t -> p (k t)")
        late_junk = arena[:, 0:D]
        pw = m[:, :, :].rearrange("p (t n) s -> p t (n s)", t=TT)

        bank = [ctx.enter_context(nc.psum_tensor(f"bank{i}", [P, 512], F32)) for i in range(8)]

        def tile_bank(n):
            return bank[n % 4]

        def job_bank(kind, j=0):
            return bank[4 + JOB[kind, j] % 4]

        loaded = [sem(f"loaded{i}") for i in range(SLOTS)]
        x_in = sem("x_in")
        vec_in = sem("vec_in")
        p_in = sem("p_in")
        rot_in = sem("rot_in")
        dec_in = sem("dec_in")
        count_in = sem("count_in")
        router_in = sem("router_in")
        bgu_in = sem("bgu_in")
        bdown_in = sem("bdown_in")
        gfin_in = sem("gfin_in")
        out_done = sem("out_done")
        tables = sem("tables")
        tiles_done = sem("tiles_done")
        jobs_done = sem("jobs_done")
        o_copied = sem("o_copied")
        dve_step = sem("dve_step")
        act_step = sem("act_step")
        pool_step = sem("pool_step")
        sumsq = sem("sumsq")
        rms_ready = sem("rms_ready")
        xs_ready = sem("xs_ready")
        hT_ready = sem("hT_ready")
        vec_ready = sem("vec_ready")
        pT_ready = sem("pT_ready")
        bias_ready = sem("bias_ready")
        q_ready = sem("q_ready")
        k_ready = sem("k_ready")
        sT_ready = sem("sT_ready")
        v_ready = sem("v_ready")
        osq_ready = sem("osq_ready")
        orms_ready = sem("orms_ready")
        pu_ready = sem("pu_ready")
        pooled_ready = sem("pooled_ready")
        ypool_ready = sem("ypool_ready")
        ga_ready = sem("ga_ready")
        ga_used = sem("ga_used")
        gb_ready = sem("gb_ready")
        gr_ready = sem("gr_ready")
        gated_o = sem("gated_o")
        merged = sem("merged")
        x1_ready = sem("x1_ready")
        sumsq2 = sem("sumsq2")
        xn_ready = sem("xn_ready")
        rms2_ready = sem("rms2_ready")
        h2T_ready = sem("h2T_ready")
        LT_ready = sem("LT_ready")
        top_ready = sem("top_ready")
        exp_ready = sem("exp_ready")
        Mb_ready = sem("Mb_ready")
        G_ready = sem("G_ready")
        GT_ready = sem("GT_ready")
        part_ready = sem("part_ready")
        resid_ready = sem("resid_ready")
        items_ready = sem("items_ready")

        slot_used = [sem(n) for n in ("glu_half", "glu_done", "lin_half", "lin_done", "down_half", "down_done")]
        glu_done, lin_done, down_done = slot_used[1], slot_used[3], slot_used[5]
        hot_ready = sem("hot_ready")
        gathered = sem("gathered")
        XT_ready = sem("XT_ready")
        bsel_ready = sem("bsel_ready")
        Cg_ready = sem("Cg_ready")
        CT_done = sem("CT_done")
        CT_ready = sem("CT_ready")
        g7_ready = sem("g7_ready")
        sig_ready = sem("sig_ready")
        gs_ready = sem("gs_ready")
        l7_ready = sem("l7_ready")
        act_ready = sem("act_ready")
        aT_done = sem("aT_done")
        aT_ready = sem("aT_ready")
        y_ready = sem("y_ready")
        moe_done = sem("moe_done")
        x2_ready = sem("x2_ready")
        sumsq3 = sem("sumsq3")
        rms3_ready = sem("rms3_ready")
        u_ready = sem("u_ready")
        pw_done = sem("pw_done")
        pw_ready = sem("pw_ready")
        uT_done = sem("uT_done")
        uT_ready = sem("uT_ready")
        gate_done = sem("gate_done")
        gate_ready = sem("gate_ready")
        x3_ready = sem("x3_ready")
        sumsq4 = sem("sumsq4")
        rms4_ready = sem("rms4_ready")
        out_ready = sem("out_ready")

        def wait_tile_free(pe, n):
            kind, j = TILES[n]
            taken, count = {"q": (q_ready, 2 * j + 2), "k": (k_ready, 2 * j + 2), "v": (v_ready, j + 1),
                            "pool": (pu_ready, j + 1), "ga": (ga_ready, j + 1), "gb": (gb_ready, j + 1),
                            "gr": (gated_o, HEADS + j + 1), "ro": (merged, j + 1), "wo": (x1_ready, j + 1)}[kind]
            pe.wait_ge(taken, count)

        def wait_job_free(pe, n):
            kind, j = JOBS[n]
            taken, count = {"xT": (hT_ready, j + 1), "vec": (vec_ready, 1), "pT": (pT_ready, 1),
                            "scores": (sT_ready, j + 1), "o": (o_copied, j + 1), "ss": (orms_ready, j + 1),
                            "ypool": (ypool_ready, 2 * j + 2), "hT": (h2T_ready, j + 1), "logits": (LT_ready, 1),
                            "logitsT": (top_ready, 1), "gT": (GT_ready, 1), "rank": (items_ready, 1)}[kind]
            pe.wait_ge(taken, count)

        def slot_of(n):
            return (N1 + n) % SLOTS

        def item_loads(n):
            return (N1 + n) // SLOTS

        block = ctx.enter_context(nc.Block())

        @block.sync
        def _(sp):
            def load_chunk(n):
                kind, j = CHUNKS[n]
                slot = ring[:, n % SLOTS, :]
                if kind in COL:
                    c = COL[kind] + HALF * j
                    src = w_in_v[:, :, c:c + HALF]
                    dst = slot.rearrange("p (k n) -> p k n", k=KT)
                elif kind == "wpool":
                    src = w_pool_v
                    dst = slot[:, 0:2048].rearrange("p (g c d) -> p g c d", g=4, c=2)
                elif kind == "ro":
                    src = w_ro_v[:, :, 256 * j:256 * j + 256]
                    dst = slot.rearrange("p (k n) -> p k n", k=16)
                else:
                    src = w_out_v[:, :, HALF * j:HALF * j + HALF]
                    dst = slot.rearrange("p (k n) -> p k n", k=KT)
                sp.dma_start(dst, src).then_inc(loaded[n % SLOTS], 16)

            def wait_used(n):
                kind, j = CHUNKS[n]
                if kind == "wpool":
                    sp.wait_ge(jobs_done, job_done("ypool", 3))
                elif kind == "ro":
                    sp.wait_ge(tiles_done, tile_done("ro", j))
                else:
                    sp.wait_ge(tiles_done, tile_done(kind, 2 * j + 1))

            def load_item(n, e):
                rows = slice(HALF * (n % 2), HALF * (n % 2) + HALF)
                cols = slice(FF * (n // 2), FF * (n // 2) + FF)
                src = w_gate_up[0, bass.ds(e, 1), rows, cols] if n < 4 else w_down[0, bass.ds(e, 1), rows, :]
                sp.dma_start(ring[:, slot_of(n), :].rearrange("p (k n) -> p k n", k=4),
                             src.rearrange("a (k p) n -> p (a k) n", p=P)).then_inc(loaded[slot_of(n)], 16)

            for t in range(TT):
                sp.dma_start(xs[:, t, :], x_v[:, t, :]).then_inc(x_in, 16)
            for n in range(N1):
                if n >= SLOTS:
                    wait_used(n - SLOTS)
                load_chunk(n)
            for n in range(SLOTS):
                wait_used(N1 - SLOTS + n)
                load_item(n, 0)
            sp.wait_ge(items_ready, 1)
            end = sp.value_load(nitems[0:1, 0:1], min_val=NE, max_val=NE * MAX_BLOCKS)
            with sp.Fori(1, end) as i:
                e = sp.snap(sp.to_reg(i & (NE - 1)), min_val=0, max_val=NE - 1)
                for n in range(SLOTS):
                    sp.wait_ge(slot_used[n], i)
                    load_item(n, e)
            for n in range(3):
                sp.wait_ge(slot_used[n], end)
                slot = ring[:, slot_of(n), :]
                if n < 2:
                    sp.dma_start(slot.rearrange("p (k n) -> p k n", k=KT),
                                 w_pg_v[:, :, HALF * n:HALF * n + HALF]).then_inc(loaded[slot_of(n)], 16)
                else:
                    sp.dma_start(slot[:, 0:2048].rearrange("p (k n) -> p k n", k=2),
                                 w_ple_v).then_inc(loaded[slot_of(n)], 16)
            for t in range(TT):
                sp.wait_ge(out_ready, t + 1)
                sp.dma_start(out_v[:, t, :], oT[:, 8 + 4 * t:12 + 4 * t, :].rearrange("p c s -> p (c s)")
                             ).then_inc(out_done, 16)
            sp.wait_ge(out_done, 16 * TT)

        @block.gpsimd
        def _(pool):
            steps = [0]

            def link(ins):
                steps[0] += 1
                ins.then_inc(pool_step, 1)
                pool.wait_ge(pool_step, steps[0])

            link(nc.gpsimd.memset(ident[:], 0.0))
            nc.gpsimd.affine_select(out=ident[:], in_=ident[:], compare_op=ALU.not_equal, fill=1.0, base=0,
                                    pattern=[[-1, P]], channel_multiplier=1).then_inc(tables, 1)
            nc.gpsimd.memset(eps_t[:], EPS).then_inc(tables, 1)
            nc.gpsimd.memset(ones[:], 1.0).then_inc(tables, 1)
            nc.gpsimd.memset(onesb[:], 1.0).then_inc(tables, 1)
            link(nc.gpsimd.memset(before[:], 1.0))
            nc.gpsimd.affine_select(out=before[:], in_=before[:], compare_op=ALU.is_gt, fill=0.0, base=0,
                                    pattern=[[1, P]], channel_multiplier=-1).then_inc(tables, 1)
            link(nc.gpsimd.memset(pick[:], 0.0))
            for c in range(3):
                nc.gpsimd.affine_select(out=pick[32 * c:32 * c + 32, :], in_=pick[32 * c:32 * c + 32, :],
                                        compare_op=ALU.not_equal, fill=1.0, base=0, pattern=[[-1, NE]],
                                        channel_multiplier=1).then_inc(tables, 1)
                pool.wait_ge(tables, 6 + c)
            nc.gpsimd.iota(slots_io[:], pattern=[[CAP, MAX_BLOCKS + 1], [0, 2], [1, CAP]], base=0,
                           channel_multiplier=0, allow_small_or_imprecise_dtypes=True).then_inc(tables, 1)
            nc.gpsimd.iota(exp_io[:], pattern=[[1, NE]], base=0, channel_multiplier=0,
                           allow_small_or_imprecise_dtypes=True).then_inc(tables, 1)
            nc.gpsimd.iota(steps64[:], pattern=[[CAP, MAX_BLOCKS]], base=0, channel_multiplier=0,
                           allow_small_or_imprecise_dtypes=True).then_inc(tables, 1)

            pool.wait_ge(jobs_done, job_done("scores", HEADS - 1))
            for b in (pu, pa, pb):
                link(nc.gpsimd.memset(b[:, :, 0:PAD], 0.0))
            pool.wait_ge(count_in, 16)
            for g, w in enumerate(WINDOWS):
                pool.wait_ge(pu_ready, g + 1)
                src, shift, n = pu, 1, 0
                while shift < w:
                    dst = (pa, pb)[n % 2]
                    link(nc.gpsimd.tensor_tensor(dst[:, :, PAD:], src[:, :, PAD:],
                                                 src[:, :, PAD - shift:PAD + S - shift], ALU.add))
                    src, shift, n = dst, 2 * shift, n + 1
                dst = (pa, pb)[n % 2]
                link(nc.gpsimd.tensor_tensor(dst[:, :, PAD:], src[:, :, PAD:],
                                             recip_count[:, g:g + 1, :].to_broadcast([P, 2, S]), ALU.mult))
                nc.gpsimd.tensor_tensor(m[:, 2 * g:2 * g + 2, :], dst[:, :, PAD:], pu[:, :, PAD:],
                                        ALU.subtract).then_inc(pooled_ready, 1)
            for j in range(4):
                pool.wait_ge(ypool_ready, 2 * j + 2)
                pool.wait_ge(ga_ready, j + 1)
                nc.gpsimd.tensor_tensor(m[:, 2 * j:2 * j + 2, :], m[:, 2 * j:2 * j + 2, :],
                                        tmp[:, j % 2, :].rearrange("p (a t) -> p a t", a=2),
                                        ALU.mult).then_inc(ga_used, 1)
            for c in range(2):
                pool.wait_ge(part_ready, c + 1)
                pool.wait_ge(xn_ready, TT)
                if c == 1:
                    pool.wait_ge(resid_ready, 1)
                nc.gpsimd.tensor_tensor(resid, xn if c == 0 else resid, parts[:, c, :, :],
                                        ALU.subtract).then_inc(resid_ready, 1)

        @block.scalar
        def _(a):
            steps = [0]

            def link(ins):
                steps[0] += 1
                ins.then_inc(act_step, 1)
                a.wait_ge(act_step, steps[0])

            for n, g in enumerate((g_mix, pool_scale, g_ffn, g_ple)):
                a.dma_start(vrow[8 * n:8 * n + 8, :], g[0].rearrange("(k p) -> k p", p=P)).then_inc(vec_in, 16)
            a.dma_start(rot, c_rot).then_inc(rot_in, 16)
            a.dma_start(dec, c_decay).then_inc(dec_in, 16)
            a.dma_start(prow.rearrange("p (t c) s -> p t (c s)", t=TT), p_v).then_inc(p_in, 16)

            for t in range(TT):
                a.wait_ge(x_in, 16 * TT)
                nc.scalar.activation(junk, xs[:, t, :], ACT.Square, accum_out=stat[:, 0, t:t + 1]
                                     ).then_inc(sumsq, 1)
                a.wait_ge(sumsq, t + 1)
            a.wait_ge(tables, 2)
            nc.scalar.activation(stat[:, 1, :], stat[:, 0, :], ACT.Sqrt, bias=eps_t[:, 0:1],
                                 scale=1.0 / D).then_inc(rms_ready, 1)

            for c in range(3):
                a.dma_start(bgu[32 * c:32 * c + 32, :], b_gate_up[0]).then_inc(bgu_in, 16)
            a.dma_start(recip_count[:], c_count).then_inc(count_in, 16)
            a.dma_start(wrt[:], w_router[0].rearrange("(k p) e -> p k e", p=P)).then_inc(router_in, 16)
            a.dma_start(brt[:], b_router[0].rearrange("(e a) -> e a", a=1)).then_inc(router_in, 16)

            def take_v(h):
                for t in range(TT):
                    a.wait_ge(tiles_done, tile_done("v", 2 * h + t))
                    if h >= 2:
                        a.wait_ge(jobs_done, job_done("o", 2 * (h - 2) + 1))
                    nc.scalar.copy(v[:, h % 2, t, :], tile_bank(TILE["v", 2 * h + t])[:]).then_inc(v_ready, 1)

            def square_o(h):
                for b in range(2):
                    a.wait_ge(jobs_done, job_done("o", 2 * h + b))
                    if h >= 1:
                        a.wait_ge(jobs_done, job_done("ss", h - 1))
                    nc.scalar.activation(osq[:, b, :, :], job_bank("o", 2 * h + b)[:].rearrange(
                        "p (a t) -> p a t", a=2), ACT.Square).then_inc(osq_ready, 1)

            def root_o(h):
                a.wait_ge(jobs_done, job_done("ss", h))
                if h >= 1:
                    a.wait_ge(gated_o, h)
                nc.scalar.activation(rr, job_bank("ss", h)[:, 0:S], ACT.Sqrt, bias=eps_t[:, 0:1],
                                     scale=1.0 / DV).then_inc(orms_ready, 1)

            take_v(0)
            take_v(1)
            square_o(0)
            take_v(2)
            root_o(0)
            square_o(1)
            take_v(3)
            root_o(1)
            square_o(2)

            def take_pool(g):
                a.wait_ge(tiles_done, tile_done("pool", g))
                a.wait_ge(pool_step, 6)
                if g >= 1:
                    a.wait_ge(pooled_ready, g)
                nc.scalar.copy(pu[:, :, PAD:], tile_bank(TILE["pool", g])[:].rearrange(
                    "p (a t) -> p a t", a=2)).then_inc(pu_ready, 1)

            take_pool(0)
            take_pool(1)
            root_o(2)
            square_o(3)
            take_pool(2)
            take_pool(3)
            root_o(3)

            def scale_ypool(g):
                a.wait_ge(jobs_done, job_done("ypool", g))
                for c in range(2):
                    n = 2 * g + c
                    nc.scalar.activation(m[:, n, :], job_bank("ypool", g)[:, S * c:S * c + S], ACT.Copy,
                                         scale=vec[:, 1, n:n + 1]).then_inc(ypool_ready, 1)

            def gate_a(j):
                a.wait_ge(tiles_done, tile_done("ga", j))
                if j >= 2:
                    a.wait_ge(ga_used, j - 1)
                nc.scalar.activation(tmp[:, j % 2, :], tile_bank(TILE["ga", j])[:], ACT.Sigmoid
                                     ).then_inc(ga_ready, 1)

            a.wait_ge(vec_ready, 1)
            gate_a(0)
            gate_a(1)
            scale_ypool(0)
            scale_ypool(1)
            gate_a(2)
            gate_a(3)
            a.wait_ge(bias_ready, 2)
            for j in range(4):
                a.wait_ge(tiles_done, tile_done("gb", j))
                nc.scalar.activation(sigB[:, 2 * j:2 * j + 2, :], tile_bank(TILE["gb", j])[:].rearrange(
                    "p (a t) -> p a t", a=2), ACT.Sigmoid).then_inc(gb_ready, 1)
                if j == 1:
                    scale_ypool(2)
                    scale_ypool(3)
            for j in range(8):
                a.wait_ge(tiles_done, tile_done("gr", j))
                if j < 2:
                    a.wait_ge(ga_used, 3 + j)
                else:
                    a.wait_ge(gated_o, HEADS + j - 1)
                nc.scalar.activation(tmp[:, j % 2, :], tile_bank(TILE["gr", j])[:], ACT.Sigmoid
                                     ).then_inc(gr_ready, 1)

            a.wait_ge(merged, 4)
            a.dma_start(bdown, b_down[0]).then_inc(bdown_in, 16)
            a.dma_start(gfin, g_final.rearrange("(a d) -> a d", a=1).to_broadcast([P, D])).then_inc(gfin_in, 16)

            for t in range(TT):
                a.wait_ge(x1_ready, 3 + t)
                nc.scalar.activation(junk, xs[:, t, :], ACT.Square, accum_out=stat[:, 2, t:t + 1]
                                     ).then_inc(sumsq2, 1)
                a.wait_ge(sumsq2, t + 1)
            nc.scalar.activation(stat[:, 3, :], stat[:, 2, :], ACT.Sqrt, bias=eps_t[:, 0:1],
                                 scale=1.0 / D).then_inc(rms2_ready, 1)
            a.wait_ge(xn_ready, TT)
            nc.scalar.copy(parts[:, 0, :, :], xn).then_inc(part_ready, 1)
            a.wait_ge(jobs_done, job_done("logits"))
            a.wait_ge(router_in, 32)
            nc.scalar.activation(LT[:], job_bank("logits")[0:NE, 0:S], ACT.Identity,
                                 bias=brt[:, 0:1]).then_inc(LT_ready, 1)
            a.wait_ge(resid_ready, 1)
            nc.scalar.copy(parts[:, 1, :, :], resid).then_inc(part_ready, 1)
            a.wait_ge(top_ready, 1)
            for t in range(TT):
                nc.scalar.activation(Eg[:, t, :], L[:, t, :], ACT.Exp, bias=stat[:, 4, t:t + 1]
                                     ).then_inc(exp_ready, 1)
            a.wait_ge(resid_ready, 2)
            nc.scalar.copy(parts[:, 2, :, :], resid).then_inc(part_ready, 1)
            a.wait_ge(jobs_done, job_done("gT"))
            nc.scalar.copy(GT[:], job_bank("gT")[0:NE, 0:S]).then_inc(GT_ready, 1)

            a.wait_ge(items_ready, 1)
            end = a.value_load(nitems[0:1, 0:1], min_val=NE, max_val=NE * MAX_BLOCKS)
            with a.Fori(0, end) as i:
                a.wait_ge(g7_ready, i + 1)
                nc.scalar.activation(gs, g7, ACT.Sigmoid, scale=ALPHA).then_inc(sig_ready, 1)
                a.wait_ge(CT_done, i + 1)
                nc.scalar.copy(CT, bank[3][:, 0:S].rearrange("p (t s) -> p t s", t=TT)).then_inc(CT_ready, 1)
                a.wait_ge(aT_done, i + 1)
                nc.scalar.copy(aT, bank[0][:].rearrange("p (j h s) -> p j h s", j=4, h=2)).then_inc(aT_ready, 1)
                a.wait_ge(down_done, i + 1)
                nc.scalar.copy(y, bank[3][:]).then_inc(y_ready, 1)

            for n in range(4):
                a.wait_ge(pw_done, n + 1)
                nc.scalar.copy(pw[:, n // 2, HALF * (n % 2):HALF * (n % 2) + HALF], bank[n][:]).then_inc(pw_ready, 1)
            for t in range(TT):
                a.wait_ge(x2_ready, 2 * t + 2)
                nc.scalar.activation(late_junk, xs[:, t, :], ACT.Square, accum_out=stat[:, 2, t:t + 1]
                                     ).then_inc(sumsq3, 1)
                a.wait_ge(sumsq3, t + 1)
                nc.scalar.activation(stat[:, 3, t:t + 1], stat[:, 2, t:t + 1], ACT.Sqrt, bias=eps_t[:, 0:1],
                                     scale=1.0 / D).then_inc(rms3_ready, 1)
            for n in range(4):
                a.wait_ge(gate_done, n + 1)
                nc.scalar.activation(tmp[:, n % 2, :] if n < 2 else sigB[:, 2 * n - 4:2 * n - 2, :].rearrange(
                    "p a t -> p (a t)"), bank[n][:], ACT.Sigmoid).then_inc(gate_ready, 1)
            for t in range(TT):
                a.wait_ge(x3_ready, 2 * t + 2)
                nc.scalar.activation(late_junk, xs[:, t, :], ACT.Square, accum_out=stat[:, 5, t:t + 1]
                                     ).then_inc(sumsq4, 1)
                a.wait_ge(sumsq4, t + 1)
                nc.scalar.activation(stat[:, 6, t:t + 1], stat[:, 5, t:t + 1], ACT.Sqrt, bias=eps_t[:, 0:1],
                                     scale=1.0 / D).then_inc(rms4_ready, 1)

        @block.vector
        def _(dve):
            steps = [0]

            def link(ins):
                steps[0] += 1
                ins.then_inc(dve_step, 1)
                dve.wait_ge(dve_step, steps[0])

            dve.wait_ge(rms_ready, 1)
            link(nc.vector.reciprocal(stat[:, 1, :], stat[:, 1, :]))
            for t in range(TT):
                nc.vector.tensor_scalar(xn[:, t, :], xs[:, t, :], stat[:, 1, t:t + 1], None,
                                        ALU.mult).then_inc(xs_ready, 1)
            dve.wait_ge(jobs_done, job_done("vec"))
            nc.vector.tensor_copy(vec[:], job_bank("vec")[:, 0:32].rearrange("p (n k) -> p n k", n=4)
                                  ).then_inc(vec_ready, 1)
            dve.wait_ge(vec_ready, 1)
            for j in range(4):
                dve.wait_ge(jobs_done, job_done("xT", j))
                nc.vector.tensor_tensor(hT[:, 2 * j:2 * j + 2, :], job_bank("xT", j)[:].rearrange(
                    "p (a t) -> p a t", a=2), vec[:, 0, 2 * j:2 * j + 2].unsqueeze(2).to_broadcast([P, 2, S]),
                    ALU.mult).then_inc(hT_ready, 1)
            dve.wait_ge(jobs_done, job_done("pT"))
            nc.vector.tensor_copy(pT[:], job_bank("pT")[:].rearrange("p (a t) -> p a t", a=2)
                                  ).then_inc(pT_ready, 1)

            dve.wait_ge(rot_in, 16)

            def rotate(kind, h, dst, ready):
                n = TILE[kind, h]
                dve.wait_ge(tiles_done, n + 1)
                if h >= 2:
                    dve.wait_ge(jobs_done, job_done("scores", h - 2))
                src = tile_bank(n)[:].rearrange("p (a t) -> p a t", a=2)
                for c in range(2):
                    ins = nc.vector.tensor_tensor(tmp[:, c, :].rearrange("p (a t) -> p a t", a=2), src,
                                                  rot[:, c:c + 1, :].to_broadcast([P, 2, S]), ALU.mult)
                    link(ins)
                nc.vector.tensor_tensor(dst[:, h % 2, 0, :], tmp[:, 0, 0:S], tmp[:, 1, S:2 * S],
                                        ALU.subtract).then_inc(ready, 1)
                nc.vector.tensor_tensor(dst[:, h % 2, 1, :], tmp[:, 0, S:2 * S], tmp[:, 1, 0:S],
                                        ALU.add).then_inc(ready, 1)
                dve.wait_ge(ready, 2 * h + 2)

            def mask_scores(h):
                dve.wait_ge(jobs_done, job_done("scores", h))
                nc.vector.tensor_tensor(sT[:, h, :], job_bank("scores", h)[:, 0:384], dec[:, h, :],
                                        ALU.mult).then_inc(sT_ready, 1)

            for h in (0, 1):
                rotate("q", h, qr, q_ready)
            for h in (0, 1):
                rotate("k", h, kr, k_ready)
            dve.wait_ge(dec_in, 16)
            mask_scores(0)
            mask_scores(1)
            for h in (2, 3):
                rotate("q", h, qr, q_ready)
            for h in (2, 3):
                rotate("k", h, kr, k_ready)
            mask_scores(2)
            mask_scores(3)

            dve.wait_ge(bgu_in, 48)
            link(nc.vector.tensor_copy(bias_parts[:], bgu))
            link(nc.vector.tensor_tensor(bgu, bgu, bias_parts[:], ALU.subtract))
            nc.vector.tensor_copy(bias_parts[32:64, :], bgu[32:64, :]).then_inc(bias_ready, 1)
            link(nc.vector.tensor_copy(bias_parts[64:96, :], bgu[64:96, :]))
            link(nc.vector.tensor_tensor(bgu[64:96, :], bgu[64:96, :], bias_parts[64:96, :], ALU.subtract))
            nc.vector.tensor_copy(bias_parts[64:96, :], bgu[64:96, :]).then_inc(bias_ready, 1)

            def copy_o(h):
                for b in range(2):
                    dve.wait_ge(osq_ready, 2 * h + b + 1)
                    c = 4 * h + 2 * b
                    nc.vector.tensor_copy(oT[:, c:c + 2, :], job_bank("o", 2 * h + b)[:].rearrange(
                        "p (a t) -> p a t", a=2)).then_inc(o_copied, 1)

            def norm_o(h):
                dve.wait_ge(orms_ready, h + 1)
                link(nc.vector.reciprocal(rr, rr))
                dve.wait_ge(o_copied, 2 * h + 2)
                nc.vector.tensor_tensor(oT[:, 4 * h:4 * h + 4, :], oT[:, 4 * h:4 * h + 4, :],
                                        rr.unsqueeze(1).to_broadcast([P, 4, S]), ALU.mult).then_inc(gated_o, 1)

            for h in range(HEADS):
                copy_o(h)
                norm_o(h)

            dve.wait_ge(gated_o, HEADS)
            for j in range(8):
                n = TILE["gr", j]
                dve.wait_ge(gr_ready, j + 1)
                link(nc.vector.tensor_tensor(tmp[:, j % 2, :], tile_bank(n)[:], tmp[:, j % 2, :], ALU.mult))
                nc.vector.tensor_tensor(oT[:, 2 * j:2 * j + 2, :], oT[:, 2 * j:2 * j + 2, :],
                                        tmp[:, j % 2, :].rearrange("p (a t) -> p a t", a=2),
                                        ALU.mult).then_inc(gated_o, 1)

            dve.wait_ge(gb_ready, 4)
            dve.wait_ge(ga_used, 4)
            for j in range(4):
                n = TILE["ro", j]
                dve.wait_ge(tiles_done, n + 1)
                two = slice(2 * j, 2 * j + 2)
                link(nc.vector.tensor_tensor(sigB[:, two, :], tile_bank(n)[:].rearrange("p (a t) -> p a t", a=2),
                                             sigB[:, two, :], ALU.mult))
                nc.vector.tensor_tensor(m[:, two, :], m[:, two, :], sigB[:, two, :], ALU.add).then_inc(merged, 1)

            for n in range(4):
                k = TILE["wo", n]
                dve.wait_ge(tiles_done, k + 1)
                cols = slice(HALF * (n // 2), HALF * (n // 2) + HALF)
                nc.vector.tensor_tensor(xs[:, n % 2, cols], xs[:, n % 2, cols], tile_bank(k)[:],
                                        ALU.add).then_inc(x1_ready, 1)

            dve.wait_ge(rms2_ready, 1)
            link(nc.vector.reciprocal(stat[:, 3, :], stat[:, 3, :]))
            for t in range(TT):
                nc.vector.tensor_scalar(xn[:, t, :], xs[:, t, :], stat[:, 3, t:t + 1], None,
                                        ALU.mult).then_inc(xn_ready, 1)
            for j in range(4):
                dve.wait_ge(jobs_done, job_done("hT", j))
                nc.vector.tensor_tensor(hT[:, 2 * j:2 * j + 2, :], job_bank("hT", j)[:].rearrange(
                    "p (a t) -> p a t", a=2), vec[:, 2, 2 * j:2 * j + 2].unsqueeze(2).to_broadcast([P, 2, S]),
                    ALU.mult).then_inc(h2T_ready, 1)

            dve.wait_ge(tables, 11)
            dve.wait_ge(jobs_done, job_done("logitsT"))
            link(nc.vector.tensor_copy(L[:], job_bank("logitsT")[:, 0:2 * NE].rearrange("p (t e) -> p t e", t=TT)))
            for t in range(TT):
                ins = nc.vector.max(top[:, t, :], L[:, t, :])
                if t < TT - 1:
                    ins.then_inc(dve_step, 1)
                    steps[0] += 1
            link(ins)
            nc.vector.tensor_scalar(stat[:, 4, :], top[:, :, 0], -1.0, None, ALU.mult).then_inc(top_ready, 1)
            for t in range(TT):
                link(nc.vector.max_index(topi[:, t, :], top[:, t, :], L[:, t, :]))
            link(nc.vector.tensor_copy(topf[:], topi[:]))
            for k in range(TOPK):
                for t in range(TT):
                    if k == 0:
                        ins = nc.vector.tensor_scalar(Msel[:, t, :], exp_io[:], topf[:, t, k:k + 1], None,
                                                      ALU.is_equal)
                    else:
                        ins = nc.vector.scalar_tensor_tensor(out=Msel[:, t, :], in0=exp_io[:],
                                                             scalar=topf[:, t, k:k + 1], in1=Msel[:, t, :],
                                                             op0=ALU.is_equal, op1=ALU.add)
                    link(ins)
            nc.vector.tensor_copy(Mb[:], Msel[:]).then_inc(Mb_ready, 1)
            dve.wait_ge(exp_ready, TT)
            link(nc.vector.tensor_tensor(Eg[:], Eg[:], Msel[:], ALU.mult))
            link(nc.vector.reduce_sum(stat[:, 7, :], Eg[:], AX_X))
            link(nc.vector.reciprocal(stat[:, 7, :], stat[:, 7, :]))
            for t in range(TT):
                nc.vector.tensor_scalar(G[:, t, :], Eg[:, t, :], stat[:, 7, t:t + 1], None,
                                        ALU.mult).then_inc(G_ready, 1)
            dve.wait_ge(jobs_done, job_done("rank"))
            rank = job_bank("rank")[:, 0:2 * NE].rearrange("p (t e) -> p t e", t=TT)
            link(nc.vector.scalar_tensor_tensor(out=pos[:], in0=rank, scalar=1.0, in1=Msel[:],
                                                op0=ALU.add, op1=ALU.mult))
            link(nc.vector.tensor_scalar(pos[:], pos[:], -1.0, None, ALU.add))
            link(nc.vector.reduce_max(nit[:, 0:1], job_bank("rank")[0:1, 2 * NE:3 * NE], AX_X))
            link(nc.vector.tensor_scalar(nit[:, 2:2 + MAX_BLOCKS], steps64[:], nit[:, 0:1], float(NE),
                                         ALU.is_lt, ALU.mult))
            link(nc.vector.reduce_sum(nit[:, 1:2], nit[:, 2:2 + MAX_BLOCKS], AX_X))
            nc.vector.tensor_copy(nitems[:], nit[:, 1:2]).then_inc(items_ready, 1)

            def one_hot(e, b):
                for t in range(TT):
                    ins = nc.vector.tensor_scalar(hot[:, t, :], slots_io[:, bass.ds(b, 1), 0, :].rearrange(
                        "p a s -> p (a s)"), pos[:, t, bass.ds(e, 1)], None, ALU.is_equal)
                    ins.then_inc(hot_ready, 1)

            def bias_pick(e):
                nc.vector.tensor_scalar(bsel[0:96, :], ones[0:96, 0:CAP], pick[:, bass.ds(e, 1)], None,
                                        ALU.mult).then_inc(bsel_ready, 1)

            def take_gathered():
                nc.vector.tensor_tensor(XT, bank[2][:].rearrange("p (k s) -> p k s", k=KT),
                                        vec[:, 2, :].unsqueeze(2).to_broadcast([P, KT, CAP]),
                                        ALU.mult).then_inc(XT_ready, 1)

            dve.wait_ge(tiles_done, len(TILES))
            nc.vector.memset(y, 0.0).then_inc(y_ready, 1)
            nc.vector.memset(CT, 0.0).then_inc(CT_ready, 1)
            one_hot(0, 0)
            bias_pick(0)
            dve.wait_ge(gathered, 1)
            take_gathered()
            dve.wait_ge(items_ready, 1)
            end = dve.value_load(nitems[0:1, 0:1], min_val=NE, max_val=NE * MAX_BLOCKS)
            with dve.Fori(0, end) as i:
                e, b = i & (NE - 1), i >> 5
                nxt = i + 1
                dve.wait_ge(CT_done, i)
                for t in range(TT):
                    nc.vector.tensor_scalar(Cg[:, t, :], slots_io[:, bass.ds(b, 1), :, :].rearrange(
                        "p a h s -> p (a h s)"), pos[:, t, bass.ds(e, 1)], G[:, t, bass.ds(e, 1)],
                        ALU.is_equal, ALU.mult).then_inc(Cg_ready, 1)
                dve.wait_ge(gathered, i + 1)
                one_hot(nxt & (NE - 1), nxt >> 5)
                dve.wait_ge(glu_done, i + 1)
                nc.vector.tensor_scalar(g7, bank[0][:], LIMIT, None, ALU.min).then_inc(g7_ready, 1)
                dve.wait_ge(sig_ready, i + 1)
                nc.vector.tensor_tensor(gs, g7, gs, ALU.mult).then_inc(gs_ready, 1)
                dve.wait_ge(lin_done, i + 1)
                nc.vector.tensor_scalar(l7, bank[1][:], LIMIT, -LIMIT, ALU.min, ALU.max).then_inc(l7_ready, 1)
                dve.wait_ge(gs_ready, i + 1)
                dve.wait_ge(l7_ready, i + 1)
                nc.vector.scalar_tensor_tensor(out=act, in0=l7, scalar=1.0, in1=gs, op0=ALU.add,
                                               op1=ALU.mult).then_inc(act_ready, 1)
                bias_pick(nxt & (NE - 1))
                dve.wait_ge(gathered, i + 2)
                take_gathered()

            for n in range(4):
                dve.wait_ge(moe_done, n + 1)
                cols = slice(HALF * (n % 2), HALF * (n % 2) + HALF)
                nc.vector.tensor_tensor(xs[:, n // 2, cols], xs[:, n // 2, cols], bank[4 + n][:],
                                        ALU.add).then_inc(x2_ready, 1)
            for t in range(TT):
                dve.wait_ge(rms3_ready, t + 1)
                link(nc.vector.reciprocal(stat[:, 3, t:t + 1], stat[:, 3, t:t + 1]))
                nc.vector.tensor_scalar(xn[:, t, :], xs[:, t, :], stat[:, 3, t:t + 1], None,
                                        ALU.mult).then_inc(u_ready, 1)
            for n in range(4):
                t, c = n // 2, n % 2
                dve.wait_ge(uT_done, n + 1)
                nc.vector.tensor_tensor(hT[:, 4 * c:4 * c + 4, P * t:P * t + P], bank[4 + n][:].rearrange(
                    "p (k s) -> p k s", k=4), vec[:, 3, 4 * c:4 * c + 4].unsqueeze(2).to_broadcast([P, 4, P]),
                    ALU.mult).then_inc(uT_ready, 1)
            dve.wait_ge(pw_ready, 4)
            for n in range(4):
                t = n // 2
                cols = slice(HALF * (n % 2), HALF * (n % 2) + HALF)
                dve.wait_ge(gate_ready, n + 1)
                src = tmp[:, n % 2, :] if n < 2 else sigB[:, 2 * n - 4:2 * n - 2, :].rearrange("p a t -> p (a t)")
                link(nc.vector.tensor_tensor(pw[:, t, cols], pw[:, t, cols], src, ALU.mult))
                nc.vector.tensor_tensor(xs[:, t, cols], xs[:, t, cols], pw[:, t, cols],
                                        ALU.add).then_inc(x3_ready, 1)
            dve.wait_ge(gfin_in, 16)
            for t in range(TT):
                dve.wait_ge(rms4_ready, t + 1)
                link(nc.vector.reciprocal(stat[:, 6, t:t + 1], stat[:, 6, t:t + 1]))
                nc.vector.scalar_tensor_tensor(out=oT[:, 8 + 4 * t:12 + 4 * t, :].rearrange("p c s -> p (c s)"),
                                               in0=xs[:, t, :], scalar=stat[:, 6, t:t + 1], in1=gfin,
                                               op0=ALU.mult, op1=ALU.mult).then_inc(out_ready, 1)

        @block.tensor
        def _(pe):
            def take_job(kind, j=0):
                n = JOB[kind, j]
                if n >= 4:
                    wait_job_free(pe, n - 4)
                return bank[4 + n % 4]

            def transposes(kind, src):
                for j in range(4):
                    dst = take_job(kind, j)
                    for a in range(2):
                        for t in range(TT):
                            k = 2 * j + a
                            last = nc.tensor.transpose(dst[:, S * a + P * t:S * a + P * t + P],
                                                       src[:, t, P * k:P * k + P], ident[:])
                    last.then_inc(jobs_done, 1)

            pe.wait_ge(tables, 4)
            pe.wait_ge(vec_in, 64)
            nc.tensor.transpose(take_job("vec")[:, 0:32], vrow[:], ident[0:32, 0:32]).then_inc(jobs_done, 1)
            pe.wait_ge(xs_ready, TT)
            transposes("xT", xn)
            pe.wait_ge(p_in, 16)
            dst = take_job("pT")
            pr = prow.rearrange("p (t c) s -> p t (c s)", t=TT)
            for c in range(2):
                for t in range(TT):
                    last = nc.tensor.transpose(dst[:, S * c + P * t:S * c + P * t + P],
                                               pr[:, t, P * c:P * c + P], ident[:])
            last.then_inc(jobs_done, 1)

            def chunk(n):
                kind, j = CHUNKS[n]
                pe.wait_ge(loaded[n % SLOTS], 16 * (n // SLOTS + 1))
                kts = 16 if kind == "ro" else KT
                w = ring[:, n % SLOTS, :].rearrange("p (k n) -> p k n", k=kts)
                src = {"ro": oT, "wo": m}.get(kind, hT)
                for b in range(1 if kind == "ro" else 2):
                    t = TILE[kind, j if kind == "ro" else 2 * j + b]
                    if t >= 4:
                        wait_tile_free(pe, t - 4)
                    dst = tile_bank(t)
                    if kind in ("v", "wo"):
                        for k in range(kts):
                            last = nc.tensor.matmul(dst[:], src[:, k, P * b:P * b + P], w[:, k, :],
                                                    start=(k == 0), stop=(k == kts - 1))
                    else:
                        for c in range(2):
                            col = P * (2 * b + c)
                            for k in range(kts):
                                last = nc.tensor.matmul(dst[:, S * c:S * c + S], w[:, k, col:col + P],
                                                        src[:, k, :], start=(k == 0), stop=(k == kts - 1))
                    last.then_inc(tiles_done, 1)

            def scores(h):
                pe.wait_ge(q_ready, 2 * h + 2)
                pe.wait_ge(k_ready, 2 * h + 2)
                dst = take_job("scores", h)
                for a in range(2):
                    nc.tensor.matmul(dst[:, 0:S], kr[:, h % 2, a, 0:P], qr[:, h % 2, a, :],
                                     start=(a == 0), stop=(a == 1))
                for a in range(2):
                    last = nc.tensor.matmul(dst[:, S:S + P], kr[:, h % 2, a, P:S], qr[:, h % 2, a, P:S],
                                            start=(a == 0), stop=(a == 1))
                last.then_inc(jobs_done, 1)

            def outputs(h):
                pe.wait_ge(sT_ready, h + 1)
                pe.wait_ge(v_ready, 2 * h + 2)
                for b in range(2):
                    dst = take_job("o", 2 * h + b)
                    for c in range(2):
                        col = P * (2 * b + c)
                        nc.tensor.matmul(dst[:, S * c:S * c + S], v[:, h % 2, 0, col:col + P], sT[:, h, 0:S],
                                         start=True, stop=False)
                        last = nc.tensor.matmul(dst[:, S * c + P:S * c + S], v[:, h % 2, 1, col:col + P],
                                                sT[:, h, S:S + P], start=False, stop=True)
                    last.then_inc(jobs_done, 1)

            def sum_squares(h):
                pe.wait_ge(osq_ready, 2 * h + 2)
                dst = take_job("ss", h)
                for n in range(4):
                    last = nc.tensor.matmul(dst[:, 0:S], ones[:], osq[:, n // 2, n % 2, :],
                                            start=(n == 0), stop=(n == 3))
                last.then_inc(jobs_done, 1)

            def pool_project(g):
                pe.wait_ge(pooled_ready, g + 1)
                n = CHUNKS.index(("wpool", 0))
                pe.wait_ge(loaded[n % SLOTS], 16 * (n // SLOTS + 1))
                w = ring[:, n % SLOTS, 0:2048].rearrange("p (g c d) -> p g c d", g=4, c=2)
                dst = take_job("ypool", g)
                for c in range(2):
                    for k in range(2):
                        last = nc.tensor.matmul(dst[:, S * c:S * c + S], w[:, g, k, P * c:P * c + P],
                                                m[:, 2 * g + k, :], start=(k == 0), stop=(k == 1))
                last.then_inc(jobs_done, 1)

            pe.wait_ge(hT_ready, 4)
            chunk(0)
            chunk(1)
            chunk(2)
            scores(0)
            scores(1)
            chunk(3)
            chunk(4)
            scores(2)
            scores(3)
            chunk(5)
            outputs(0)
            chunk(6)
            sum_squares(0)
            outputs(1)
            chunk(7)
            sum_squares(1)
            outputs(2)
            chunk(9)
            sum_squares(2)
            outputs(3)
            chunk(10)
            sum_squares(3)
            chunk(11)
            pool_project(0)
            pool_project(1)
            chunk(12)
            chunk(13)
            pool_project(2)
            pool_project(3)
            for n in range(14, 19):
                chunk(n)
            pe.wait_ge(gated_o, HEADS + 8)
            for n in range(19, 23):
                chunk(n)
            pe.wait_ge(merged, 4)
            chunk(23)
            chunk(24)

            pe.wait_ge(xn_ready, TT)
            transposes("hT", xn)
            pe.wait_ge(h2T_ready, 4)
            pe.wait_ge(router_in, 32)
            dst = take_job("logits")
            for k in range(KT):
                last = nc.tensor.matmul(dst[0:NE, 0:S], wrt[:, k, :], hT[:, k, :],
                                        start=(k == 0), stop=(k == KT - 1))
            last.then_inc(jobs_done, 1)
            pe.wait_ge(LT_ready, 1)
            dst = take_job("logitsT")
            for t in range(TT):
                last = nc.tensor.transpose(dst[:, NE * t:NE * t + NE], LT[:, P * t:P * t + P], ident[0:NE, 0:NE])
            last.then_inc(jobs_done, 1)
            pe.wait_ge(G_ready, TT)
            dst = take_job("gT")
            for t in range(TT):
                last = nc.tensor.transpose(dst[0:NE, P * t:P * t + P], G[:, t, :], ident[:])
            last.then_inc(jobs_done, 1)
            pe.wait_ge(Mb_ready, 1)
            pe.wait_ge(tables, 11)
            dst = take_job("rank")
            for n, terms in enumerate((((before, 0),), ((onesb, 0), (before, 1)), ((onesb, 0), (onesb, 1)))):
                for k, (mat, t) in enumerate(terms):
                    last = nc.tensor.matmul(dst[:, NE * n:NE * n + NE], mat[:], Mb[:, t, :],
                                            start=(k == 0), stop=(k == len(terms) - 1))
            last.then_inc(jobs_done, 1)

            def gather():
                for k in range(KT):
                    for c in range(3):
                        for t in range(TT):
                            last = nc.tensor.matmul(bank[2][:, CAP * k:CAP * k + CAP],
                                                    parts[:, c, t, P * k:P * k + P], hot[:, t, :],
                                                    start=(c == 0 and t == 0), stop=(c == 2 and t == TT - 1))
                last.then_inc(gathered, 1)

            def combine(final):
                for t in range(TT):
                    for h in range(2):
                        last = nc.tensor.matmul(bank[4 + 2 * t + h][:], CT[CAP * h:CAP * h + CAP, t, :],
                                                y[CAP * h:CAP * h + CAP, :], start=False, stop=final,
                                                skip_group_check=True)
                        if final:
                            last.then_inc(moe_done, 1)

            pe.wait_ge(part_ready, 3)
            pe.wait_ge(hot_ready, TT)
            gather()
            pe.wait_ge(bdown_in, 16)
            pe.wait_ge(GT_ready, 1)
            pe.wait_ge(items_ready, 1)
            for t in range(TT):
                for h in range(2):
                    nc.tensor.matmul(bank[4 + 2 * t + h][:], GT[:, P * t:P * t + P],
                                     bdown[:, HALF * h:HALF * h + HALF], start=True, stop=False,
                                     skip_group_check=True)
            pe.wait_ge(bias_ready, 2)
            end = pe.value_load(nitems[0:1, 0:1], min_val=NE, max_val=NE * MAX_BLOCKS)
            with pe.Fori(0, end) as i:
                def up(first, dst):
                    for h in range(2):
                        nc.tensor.matmul(dst[CAP * h:CAP * h + CAP, :], bsel[0:96, :],
                                         bias_parts[:, FF * (first // 2) + HALF * h:FF * (first // 2) + HALF * (h + 1)],
                                         start=True, stop=False)
                    for c in range(2):
                        n = first + c
                        w = ring[:, slot_of(n), :].rearrange("p (k n) -> p k n", k=4)
                        pe.wait_ge(loaded[slot_of(n)], 16 * (item_loads(n) + 1) + 16 * i)
                        for k in range(4):
                            for h in range(2):
                                last = nc.tensor.matmul(dst[CAP * h:CAP * h + CAP, :], XT[:, 4 * c + k, :],
                                                        w[:, k, HALF * h:HALF * h + HALF],
                                                        start=False, stop=(c == 1 and k == 3))
                        last.then_inc(slot_used[n], 1)

                pe.wait_ge(XT_ready, i + 1)
                pe.wait_ge(bsel_ready, i + 1)
                up(0, bank[0])
                pe.wait_ge(y_ready, i + 1)
                pe.wait_ge(CT_ready, i + 1)
                combine(False)
                up(2, bank[1])
                pe.wait_ge(Cg_ready, 2 * i + 2)
                for t in range(TT):
                    last = nc.tensor.transpose(bank[3][:, P * t:P * t + P], Cg[:, t, :], ident[:])
                last.then_inc(CT_done, 1)
                pe.wait_ge(hot_ready, 2 * i + 4)
                gather()
                pe.wait_ge(act_ready, i + 1)
                for j in range(4):
                    last = nc.tensor.transpose(bank[0][:, P * j:P * j + P], act[:, P * j:P * j + P], ident[:])
                last.then_inc(aT_done, 1)
                pe.wait_ge(aT_ready, i + 1)
                pe.wait_ge(CT_ready, i + 2)
                for c in range(2):
                    n = 4 + c
                    w = ring[:, slot_of(n), :].rearrange("p (k n) -> p k n", k=4)
                    pe.wait_ge(loaded[slot_of(n)], 16 * (item_loads(n) + 1) + 16 * i)
                    for k in range(4):
                        for h in range(2):
                            last = nc.tensor.matmul(bank[3][CAP * h:CAP * h + CAP, :], aT[:, k, c, :],
                                                    w[:, k, HALF * h:HALF * h + HALF],
                                                    start=(c == 0 and k == 0), stop=(c == 1 and k == 3))
                    last.then_inc(slot_used[n], 1)
            pe.wait_ge(y_ready, end + 1)
            combine(True)

            pe.wait_ge(XT_ready, end + 1)
            pe.wait_ge(pT_ready, 1)
            pe.wait_ge(loaded[slot_of(2)], 16 * (item_loads(2) + 1) + 16 * end)
            w = ring[:, slot_of(2), 0:2048].rearrange("p (k n) -> p k n", k=2)
            for n in range(4):
                t, h = n // 2, n % 2
                for k in range(2):
                    last = nc.tensor.matmul(bank[n][:], pT[:, k, P * t:P * t + P], w[:, k, HALF * h:HALF * h + HALF],
                                            start=(k == 0), stop=(k == 1))
                last.then_inc(pw_done, 1)
            for n in range(4):
                t, c = n // 2, n % 2
                pe.wait_ge(x2_ready, n + 1)
                pe.wait_ge(u_ready, t + 1)
                for k in range(4):
                    col = P * (4 * c + k)
                    last = nc.tensor.transpose(bank[4 + n][:, P * k:P * k + P], xn[:, t, col:col + P], ident[:])
                last.then_inc(uT_done, 1)
            for n in range(4):
                t, h = n // 2, n % 2
                pe.wait_ge(uT_ready, 2 * t + 2)
                pe.wait_ge(pw_ready, n + 1)
                pe.wait_ge(loaded[slot_of(h)], 16 * (item_loads(h) + 1) + 16 * end)
                w = ring[:, slot_of(h), :].rearrange("p (k n) -> p k n", k=KT)
                for k in range(KT):
                    last = nc.tensor.matmul(bank[n][:], hT[:, k, P * t:P * t + P], w[:, k, :],
                                            start=(k == 0), stop=(k == KT - 1))
                last.then_inc(gate_done, 1)


def constants():
    half = D // HEADS // 2
    inv = np.power(np.float32(10000.0), -np.linspace(0.0, 1.0, half, dtype=np.float32)).astype(np.float32)
    ang = (inv[:, None] * np.arange(S, dtype=np.float32)[None, :]).astype(np.float64)
    rot = np.stack([np.cos(ang), np.sin(ang)], axis=1).astype(np.float32)
    tok = np.arange(S)
    gap = np.abs(tok[:, None] - tok[None, :])
    seen = tok[:, None] // CHUNK <= tok[None, :] // CHUNK
    decay = np.empty((P, HEADS, S + P), np.float32)
    for h in range(HEADS):
        full = np.where(seen, np.exp(np.log(1.0 - 2.0 ** (-5.0 - h)) * gap), 0.0) * (D // HEADS) ** -0.5
        decay[:, h, :S] = full[:P]
        decay[:, h, S:] = full[P:, P:]
    count = np.stack([1.0 / np.minimum(tok + 1.0, w) for w in WINDOWS]).astype(np.float32)
    return {"c_rot": rot, "c_decay": decay, "c_count": np.ascontiguousarray(np.broadcast_to(count, (P, 4, S)))}


_INS = ["x", "p", "g_mix", "w_in", "w_pool", "pool_scale", "w_ret_o", "w_out", "g_ffn", "w_router", "b_router",
        "w_gate_up", "b_gate_up", "w_down", "b_down", "g_ple", "w_ple_gate", "w_ple", "g_final"]


def kernel(**inputs):
    import concourse.bacc as bacc
    from concourse.bass_utils import run_bass_kernel_spmd

    nc = bacc.Bacc("TRN2", target_bir_lowering=False, num_devices=1)
    arrays, args = {}, []
    values = {name: np.ascontiguousarray(inputs[name]) for name in _INS} | constants()
    for name, a in values.items():
        arrays[f"in_{name}_dram"] = a
        args.append(nc.dram_tensor(f"in_{name}_dram", a.shape, mybir.dt.from_np(a.dtype), kind="ExternalInput").ap())
    args.append(nc.dram_tensor("out_dram", (1, S, D), F32, kind="ExternalOutput").ap())
    build_kernel(nc, *args)
    r = run_bass_kernel_spmd(nc, [arrays], core_ids=[0])
    return r.results[0]["out_dram"]
```

```python
from contextlib import ExitStack

import numpy as np

import concourse.bass as bass
from concourse import mybir

F32 = mybir.dt.float32
BF16 = mybir.dt.bfloat16
F32R = mybir.dt.float32r
I32 = mybir.dt.int32
U32 = mybir.dt.uint32
ALU = mybir.AluOpType
ACT = mybir.ActivationFunctionType
AX_X = mybir.AxisListType.X

P = 128
D = 1024
S = 256
KT = D // P
TT = S // P
PLE = 256
HEADS = 4
DV = 2 * D // HEADS
NE = 32
TOPK = 4
FF = 1024
CHUNK = 64
EPS = 1e-6
ALPHA = 1.702
LIMIT = 7.0
WINDOWS = (2, 4, 8, 16)
PAD = max(WINDOWS)
HALF = 512
CAP = 64
MAX_BLOCKS = S // CAP
SLOTS = 6
SLOT = 4096

COL = {"pool": 0, "q": D, "k": 2 * D, "v": 3 * D, "gr": 5 * D, "ga": 7 * D, "gb": 8 * D}

CHUNKS = ([("q", 0), ("k", 0), ("q", 1), ("k", 1)] + [("v", h) for h in range(HEADS)]
          + [("pool", j) for j in range(2)] + [("gr", j) for j in range(4)]
          + [(k, j) for k in ("ga", "gb") for j in range(2)]
          + [("ro", j) for j in range(4)] + [("wo", j) for j in range(2)])
N1 = len(CHUNKS)
TILES = []
for _kind, _j in CHUNKS:
    TILES += [(_kind, _j)] if _kind == "ro" else [(_kind, 2 * _j), (_kind, 2 * _j + 1)]
TILE = {x: n for n, x in enumerate(TILES)}

JOBS = [("vec", 0)] + [("xT", j) for j in range(4)] + [("pT", 0)]
for _h in range(HEADS):
    JOBS.append(("scores", _h))
for _h in range(HEADS):
    JOBS += [("o", 2 * _h), ("o", 2 * _h + 1), ("ss", _h)]
JOBS += [("ypool", g) for g in range(4)]
JOBS += [("hT", 0), ("hT", 1), ("logits", 0), ("hT", 2), ("hT", 3), ("logits", 1), ("logitsT", 0), ("logitsT", 1),
         ("rank", 0), ("gT", 0)]
JOB = {x: n for n, x in enumerate(JOBS)}


def job_done(kind, j=0):
    return JOB[kind, j] + 1


def tile_done(kind, j=0):
    return TILE[kind, j] + 1


def chunk_done(n):
    kind, j = CHUNKS[n]
    return tile_done(kind, j if kind == "ro" else 2 * j + 1)


def build_kernel(nc, x, p, g_mix, w_in, w_pool, pool_scale, w_ret_o, w_out, g_ffn, w_router, b_router,
                 w_gate_up, b_gate_up, w_down, b_down, g_ple, w_ple_gate, w_ple, g_final,
                 c_rot, c_decay, c_count, out):
    x_v = x[0].rearrange("(t p) d -> p t d", p=P)
    out_v = out[0].rearrange("(t p) d -> p t d", p=P)
    p_v = p[0, 0].rearrange("(t p) d -> p t d", p=P)
    w_in_v = w_in[0].rearrange("(k p) n -> p k n", p=P)
    w_pool_v = w_pool[0].rearrange("g (c p) d -> p g c d", p=P)
    w_ro_v = w_ret_o[0].rearrange("(k p) n -> p k n", p=P)
    w_out_v = w_out[0].rearrange("(k p) n -> p k n", p=P)
    w_pg_v = w_ple_gate[0].rearrange("(k p) n -> p k n", p=P)
    w_ple_v = w_ple[0].rearrange("(k p) n -> p k n", p=P)

    with ExitStack() as ctx:
        def sb(name, shape, dt=F32):
            return ctx.enter_context(nc.sbuf_tensor(name, shape, dt))

        def sem(name):
            return ctx.enter_context(nc.semaphore(name))

        def next_address():
            return -(-nc.sbuf_base // 32) * 32

        ring_at = next_address()
        ring = sb("ring", [P, SLOTS, SLOT])

        def over(name, shape, at):
            return nc.alloc_sbuf_tensor_at(name, shape, F32R, offset=at)

        w_hi = [over(f"w_hi{b}", [P, SLOT], ring_at + 4 * SLOT * (2 + 2 * b)) for b in range(2)]
        w_lo = [over(f"w_lo{b}", [P, SLOT], ring_at + 4 * SLOT * (3 + 2 * b)) for b in range(2)]
        xs = sb("xs", [P, TT, D])
        h_hi = sb("h_hi", [P, KT, S], F32R)
        h_lo = sb("h_lo", [P, KT, S], F32R)
        m = sb("m", [P, KT, S])
        sigB = sb("sigB", [P, KT, S])
        o_at = next_address()
        oT = sb("oT", [P, 16, S])
        arena_at = next_address()
        arena = sb("arena", [P, 9312])
        o_hi = over("o_hi", [P, 16, S], o_at)
        o_lo = over("o_lo", [P, 16, S], arena_at)
        bias_parts = sb("bias_parts", [96, 2 * FF], BF16)
        wrt = sb("wrt", [P, KT, NE])
        pT = sb("pT", [P, 2, S])
        ident = sb("ident", [P, P])
        ones = sb("ones", [P, P])
        onesb = sb("onesb", [P, P], BF16)
        before = sb("before", [P, P], BF16)
        pick = sb("pick", [96, NE])
        slots_io = sb("slots_io", [P, MAX_BLOCKS + 1, 2, CAP])
        exp_io = sb("exp_io", [P, NE])
        steps64 = sb("steps64", [1, MAX_BLOCKS])
        eps_t = sb("eps_t", [P, 1])
        vrow = sb("vrow", [32, P])
        vec = sb("vec", [P, 4, KT])
        brt = sb("brt", [NE, 1])
        stat = sb("stat", [P, 10, TT])
        scrap = sb("scrap", [P, 1])
        L = sb("L", [P, TT, NE])
        top = sb("top", [P, TT, 8])
        topi = sb("topi", [P, TT, 8], U32)
        topf = sb("topf", [P, TT, 8])
        Msel = sb("Msel", [P, TT, NE])
        Mb = sb("Mb", [P, TT, NE], BF16)
        Eg = sb("Eg", [P, TT, NE])
        G = sb("G", [P, TT, NE])
        pos = sb("pos", [P, TT, NE])
        nit = sb("nit", [1, 8])
        nitems = sb("nitems", [1, 1], I32)

        cut = [0]

        def part(words):
            cut[0] += words
            assert cut[0] <= 9312
            return arena[:, cut[0] - words:cut[0]]

        v = part(2048).rearrange("p (b t n) -> p b t n", b=2, t=TT)
        sT = part(1536).rearrange("p (h n) -> p h n", h=HEADS)
        dec = part(1536).rearrange("p (h n) -> p h n", h=HEADS)
        rot = part(512).rearrange("p (a t) -> p a t", a=2)
        osq = part(1024).rearrange("p (b a t) -> p b a t", b=2, a=2)
        rr = part(256)
        start_rot = cut[0]
        qr = part(1024).rearrange("p (b a t) -> p b a t", b=2, a=2)
        kr = part(1024).rearrange("p (b a t) -> p b a t", b=2, a=2)
        cut[0] = start_rot
        pu = part(4 * (PAD + S)).rearrange("p (b a t) -> p b a t", b=2, a=2)
        pa = part(2 * (PAD + S)).rearrange("p (a t) -> p a t", a=2)
        pb = part(2 * (PAD + S)).rearrange("p (a t) -> p a t", a=2)
        recip_count = sb("recip_count", [P, 4, PAD])
        cut[0] = 0
        parts = part(3072).bitcast(BF16).rearrange("p (c t d) -> p c t d", c=3, t=TT)
        resid = part(2048).rearrange("p (t d) -> p t d", t=TT)
        XT = part(512).rearrange("p (k s) -> p k s", k=KT)
        Cg = part(256).rearrange("p (t s) -> p t s", t=TT)
        CT = part(256).rearrange("p (t s) -> p t s", t=TT)
        hot = part(64).bitcast(BF16).rearrange("p (t s) -> p t s", t=TT)
        bsel = part(32).bitcast(BF16)
        g7, gs, l7, act = part(512), part(512), part(512), part(512)
        aT = part(512).rearrange("p (j h s) -> p j h s", j=4, h=2)
        y = part(512)
        tmp = sb("tmp", [P, 2, 512])
        LT = tmp[0:NE, 0, 0:S]
        GT = tmp[0:NE, 1, 0:S]
        bgu = sigB[0:96].rearrange("p k t -> p (k t)")
        wpool = sigB[:].rearrange("p (g c) d -> p g c d", g=4)
        prow = m[:, 0:2, :]
        xn = oT[:, 0:8, :].rearrange("p (t c) s -> p t (c s)", t=TT)
        junk = oT[:, 8:12, :].rearrange("p c s -> p (c s)")
        bdown = sigB[0:NE, 0:4, :].rearrange("p k t -> p (k t)")
        gfin = sigB[:, 4:8, :].rearrange("p k t -> p (k t)")
        late_junk = arena[:, 0:D]
        uT = arena[:, 2048:4096].rearrange("p (k t) -> p k t", k=KT)
        h2T = m
        pw = m[:, :, :].rearrange("p (t n) s -> p t (n s)", t=TT)

        bank = [ctx.enter_context(nc.psum_tensor(f"bank{i}", [P, 512], F32)) for i in range(8)]

        def tile_bank(n):
            return bank[n % 4]

        def job_bank(kind, j=0):
            return bank[4 + JOB[kind, j] % 4]

        loaded = [sem(f"loaded{i}") for i in range(SLOTS)]
        x_in = [sem(f"x_in{t}") for t in range(TT)]
        wpool_in = sem("wpool_in")
        hi_ready = sem("hi_ready")
        lo_ready = sem("lo_ready")
        stats_ready = sem("stats_ready")
        warm = sem("warm")
        vec_in = sem("vec_in")
        p_in = sem("p_in")
        rot_in = sem("rot_in")
        dec_in = sem("dec_in")
        count_in = sem("count_in")
        router_in = sem("router_in")
        bgu_in = sem("bgu_in")
        bdown_in = sem("bdown_in")
        gfin_in = sem("gfin_in")
        out_done = sem("out_done")
        tables = sem("tables")
        tiles_done = sem("tiles_done")
        jobs_done = sem("jobs_done")
        o_copied = sem("o_copied")
        dve_step = sem("dve_step")
        act_step = sem("act_step")
        pool_step = sem("pool_step")
        sumsq = sem("sumsq")
        rms_ready = sem("rms_ready")
        xs_ready = sem("xs_ready")
        hT_ready = sem("hT_ready")
        vec_ready = sem("vec_ready")
        pT_ready = sem("pT_ready")
        bias_ready = sem("bias_ready")
        q_ready = sem("q_ready")
        k_ready = sem("k_ready")
        sT_ready = sem("sT_ready")
        v_ready = sem("v_ready")
        osq_ready = sem("osq_ready")
        orms_ready = sem("orms_ready")
        pu_ready = sem("pu_ready")
        pooled_ready = sem("pooled_ready")
        ypool_ready = sem("ypool_ready")
        ga_ready = sem("ga_ready")
        ga_used = sem("ga_used")
        gb_ready = sem("gb_ready")
        gr_ready = sem("gr_ready")
        gated_o = sem("gated_o")
        merged = sem("merged")
        x1_ready = sem("x1_ready")
        sumsq2 = sem("sumsq2")
        xn_ready = sem("xn_ready")
        rms2_ready = sem("rms2_ready")
        h2T_ready = sem("h2T_ready")
        LT_ready = sem("LT_ready")
        top_ready = sem("top_ready")
        exp_ready = sem("exp_ready")
        Mb_ready = sem("Mb_ready")
        G_ready = sem("G_ready")
        GT_ready = sem("GT_ready")
        part_ready = sem("part_ready")
        resid_ready = sem("resid_ready")
        items_ready = sem("items_ready")

        slot_used = [sem(n) for n in ("glu_half", "glu_done", "lin_half", "lin_done", "down_half", "down_done")]
        glu_done, lin_done, down_done = slot_used[1], slot_used[3], slot_used[5]
        hot_ready = sem("hot_ready")
        gathered = sem("gathered")
        XT_ready = sem("XT_ready")
        bsel_ready = sem("bsel_ready")
        Cg_ready = sem("Cg_ready")
        CT_done = sem("CT_done")
        CT_ready = sem("CT_ready")
        g7_ready = sem("g7_ready")
        sig_ready = sem("sig_ready")
        gs_ready = sem("gs_ready")
        l7_ready = sem("l7_ready")
        act_ready = sem("act_ready")
        aT_done = sem("aT_done")
        aT_ready = sem("aT_ready")
        y_ready = sem("y_ready")
        moe_done = sem("moe_done")
        x2_ready = sem("x2_ready")
        sumsq3 = sem("sumsq3")
        rms3_ready = sem("rms3_ready")
        u_ready = sem("u_ready")
        pw_done = sem("pw_done")
        pw_ready = sem("pw_ready")
        uT_done = sem("uT_done")
        uT_ready = sem("uT_ready")
        gate_done = sem("gate_done")
        gate_ready = sem("gate_ready")
        x3_ready = sem("x3_ready")
        sumsq4 = sem("sumsq4")
        rms4_ready = sem("rms4_ready")
        out_ready = sem("out_ready")

        def wait_tile_free(pe, n):
            kind, j = TILES[n]
            taken, count = {"q": (q_ready, 2 * j + 2), "k": (k_ready, 2 * j + 2), "v": (v_ready, j + 1),
                            "pool": (pu_ready, j + 1), "ga": (ga_ready, j + 1), "gb": (gb_ready, j + 1),
                            "gr": (gated_o, HEADS + j + 1), "ro": (merged, j + 1), "wo": (x1_ready, j + 1)}[kind]
            pe.wait_ge(taken, count)

        def wait_job_free(pe, n):
            kind, j = JOBS[n]
            taken, count = {"xT": (hT_ready, j + 1), "vec": (vec_ready, 1), "pT": (pT_ready, 1),
                            "scores": (sT_ready, j + 1), "o": (o_copied, j + 1), "ss": (orms_ready, j + 1),
                            "ypool": (ypool_ready, 2 * j + 2), "hT": (h2T_ready, j + 1), "logits": (LT_ready, j + 1),
                            "logitsT": (top_ready, j + 1), "gT": (GT_ready, 1), "rank": (items_ready, 1)}[kind]
            pe.wait_ge(taken, count)

        def chunk_halves(n, raw):
            if CHUNKS[n][0] == "ro":
                v3 = raw.rearrange("p (k n) -> p k n", k=16)
                return [v3[:, 8 * b:8 * b + 8, :] for b in range(2)]
            v3 = raw.rearrange("p (k n) -> p k n", k=KT)
            return [v3[:, :, 256 * b:256 * b + 256] for b in range(2)]

        def item_loads(n):
            return N1 // 2 if n < 2 else 0

        block = ctx.enter_context(nc.Block())

        @block.sync
        def _(sp):
            def load_chunk(n):
                kind, j = CHUNKS[n]
                slot = ring[:, n % 2, :]
                if kind in COL:
                    c = COL[kind] + HALF * j
                    src, kts = w_in_v[:, :, c:c + HALF], KT
                elif kind == "ro":
                    src, kts = w_ro_v[:, :, 256 * j:256 * j + 256], 16
                else:
                    src, kts = w_out_v[:, :, HALF * j:HALF * j + HALF], KT
                if n >= 2:
                    sp.wait_ge(lo_ready, 2 * (n - 2) + 2)
                sp.dma_start(slot.rearrange("p (k n) -> p k n", k=kts), src).then_inc(loaded[n % 2], 16)

            def load_item(n, e):
                rows = slice(HALF * (n % 2), HALF * (n % 2) + HALF)
                cols = slice(FF * (n // 2), FF * (n // 2) + FF)
                src = w_gate_up[0, bass.ds(e, 1), rows, cols] if n < 4 else w_down[0, bass.ds(e, 1), rows, :]
                sp.dma_start(ring[:, n, :].rearrange("p (k n) -> p k n", k=4),
                             src.rearrange("a (k p) n -> p (a k) n", p=P)).then_inc(loaded[n], 16)

            for t in range(TT):
                sp.dma_start(xs[:, t, :], x_v[:, t, :]).then_inc(x_in[t], 16)
            for n, g in enumerate((g_mix, pool_scale, g_ffn, g_ple)):
                sp.dma_start(vrow[8 * n:8 * n + 8, :], g[0].rearrange("(k p) -> k p", p=P)).then_inc(vec_in, 16)
            load_chunk(0)
            sp.dma_start(rot, c_rot).then_inc(rot_in, 16)
            load_chunk(1)
            sp.dma_start(dec, c_decay).then_inc(dec_in, 16)
            for n in range(2, N1):
                load_chunk(n)
                if CHUNKS[n] == ("pool", 1):
                    sp.wait_ge(bias_ready, 2)
                    sp.dma_start(wpool, w_pool_v).then_inc(wpool_in, 16)
            for n in range(SLOTS):
                if n < 2:
                    sp.wait_ge(lo_ready, 2 * (N1 - 2 + n) + 2)
                else:
                    sp.wait_ge(tiles_done, chunk_done(N1 - 2 + (n - 2) // 2))
                load_item(n, 0)
            sp.wait_ge(items_ready, 1)
            end = sp.value_load(nitems[0:1, 0:1], min_val=NE, max_val=NE * MAX_BLOCKS)
            with sp.Fori(1, end) as i:
                e = sp.snap(sp.to_reg(i & (NE - 1)), min_val=0, max_val=NE - 1)
                for n in range(SLOTS):
                    sp.wait_ge(slot_used[n], i)
                    load_item(n, e)
            for n in range(3):
                sp.wait_ge(slot_used[n], end)
                slot = ring[:, n, :]
                if n == 0:
                    sp.dma_start(slot[:, 0:2048].rearrange("p (k n) -> p k n", k=2),
                                 w_ple_v).then_inc(loaded[n], 16)
                else:
                    sp.dma_start(slot.rearrange("p (k n) -> p k n", k=KT),
                                 w_pg_v[:, :, HALF * (n - 1):HALF * n]).then_inc(loaded[n], 16)
            for t in range(TT):
                sp.wait_ge(out_ready, t + 1)
                sp.dma_start(out_v[:, t, :], oT[:, 8 + 4 * t:12 + 4 * t, :].rearrange("p c s -> p (c s)")
                             ).then_inc(out_done, 16)
            sp.wait_ge(out_done, 16 * TT)

        @block.gpsimd
        def _(pool):
            steps = [0]

            def link(ins):
                steps[0] += 1
                ins.then_inc(pool_step, 1)
                pool.wait_ge(pool_step, steps[0])

            link(nc.gpsimd.memset(ident[:], 0.0))
            nc.gpsimd.affine_select(out=ident[:], in_=ident[:], compare_op=ALU.not_equal, fill=1.0, base=0,
                                    pattern=[[-1, P]], channel_multiplier=1).then_inc(tables, 1)
            nc.gpsimd.memset(eps_t[:], EPS).then_inc(tables, 1)
            nc.gpsimd.memset(ones[:], 1.0).then_inc(tables, 1)
            nc.gpsimd.memset(onesb[:], 1.0).then_inc(tables, 1)
            link(nc.gpsimd.memset(before[:], 1.0))
            nc.gpsimd.affine_select(out=before[:], in_=before[:], compare_op=ALU.is_gt, fill=0.0, base=0,
                                    pattern=[[1, P]], channel_multiplier=-1).then_inc(tables, 1)
            link(nc.gpsimd.memset(pick[:], 0.0))
            for c in range(3):
                nc.gpsimd.affine_select(out=pick[32 * c:32 * c + 32, :], in_=pick[32 * c:32 * c + 32, :],
                                        compare_op=ALU.not_equal, fill=1.0, base=0, pattern=[[-1, NE]],
                                        channel_multiplier=1).then_inc(tables, 1)
                pool.wait_ge(tables, 6 + c)
            nc.gpsimd.iota(slots_io[:], pattern=[[CAP, MAX_BLOCKS + 1], [0, 2], [1, CAP]], base=0,
                           channel_multiplier=0, allow_small_or_imprecise_dtypes=True).then_inc(tables, 1)
            nc.gpsimd.iota(exp_io[:], pattern=[[1, NE]], base=0, channel_multiplier=0,
                           allow_small_or_imprecise_dtypes=True).then_inc(tables, 1)
            nc.gpsimd.iota(steps64[:], pattern=[[CAP, MAX_BLOCKS]], base=0, channel_multiplier=0,
                           allow_small_or_imprecise_dtypes=True).then_inc(tables, 1)

            pool.wait_ge(jobs_done, job_done("scores", HEADS - 1))
            for b in (pu[:, 0], pu[:, 1], pa, pb):
                link(nc.gpsimd.memset(b[:, :, 0:PAD], 0.0))
            pool.wait_ge(count_in, 16)
            for g, w in enumerate(WINDOWS):
                pool.wait_ge(pu_ready, g + 1)
                if g >= 1:
                    pool.wait_ge(pooled_ready, g)
                u = pu[:, g % 2]
                src, shift, n = u, 1, 0
                while shift < w:
                    dst = (pa, pb)[n % 2]
                    link(nc.gpsimd.tensor_tensor(dst[:, :, PAD:], src[:, :, PAD:],
                                                 src[:, :, PAD - shift:PAD + S - shift], ALU.add))
                    src, shift, n = dst, 2 * shift, n + 1
                dst = (pa, pb)[n % 2]
                link(nc.gpsimd.tensor_tensor(dst[:, :, PAD:2 * PAD], src[:, :, PAD:2 * PAD],
                                             recip_count[:, g:g + 1, :].to_broadcast([P, 2, PAD]), ALU.mult))
                link(nc.gpsimd.tensor_scalar(dst[:, :, 2 * PAD:], src[:, :, 2 * PAD:], 1.0 / w, None, ALU.mult))
                nc.gpsimd.tensor_tensor(m[:, 2 * g:2 * g + 2, :], dst[:, :, PAD:], u[:, :, PAD:],
                                        ALU.subtract).then_inc(pooled_ready, 1)
            for j in range(4):
                pool.wait_ge(ypool_ready, 2 * j + 2)
                pool.wait_ge(ga_ready, j + 1)
                nc.gpsimd.tensor_tensor(m[:, 2 * j:2 * j + 2, :], m[:, 2 * j:2 * j + 2, :],
                                        tmp[:, j % 2, :].rearrange("p (a t) -> p a t", a=2),
                                        ALU.mult).then_inc(ga_used, 1)
            for n, (c, t) in enumerate(((0, 0), (0, 1), (1, 0), (1, 1))):
                pool.wait_ge(part_ready, n + 1)
                if c == 1:
                    pool.wait_ge(resid_ready, t + 1)
                nc.gpsimd.tensor_tensor(resid[:, t, :], xn[:, t, :] if c == 0 else resid[:, t, :],
                                        parts[:, c, t, :], ALU.subtract).then_inc(resid_ready, 1)

        @block.scalar
        def _(a):
            steps = [0]

            def link(ins):
                steps[0] += 1
                ins.then_inc(act_step, 1)
                a.wait_ge(act_step, steps[0])

            a.dma_start(recip_count[:], c_count).then_inc(count_in, 16)
            a.dma_start(prow.rearrange("p (t c) s -> p t (c s)", t=TT), p_v).then_inc(p_in, 16)

            def square(src, row, t, done, scratch):
                nc.scalar.activation(scratch, src, ACT.Square, accum_out=stat[:, row, t:t + 1]).then_inc(done, 1)

            def root(row, t, done):
                nc.scalar.activation(stat[:, row + 1, t:t + 1], stat[:, row, t:t + 1], ACT.Sqrt,
                                     bias=eps_t[:, 0:1], scale=1.0 / D).then_inc(done, 1)

            def load_table(func):
                nc.scalar.activation(scrap[:], eps_t[:], func).then_inc(warm, 1)

            a.wait_ge(tables, 2)
            load_table(ACT.Sqrt)
            for t in range(TT):
                a.wait_ge(x_in[t], 16)
                square(xs[:, t, :], 0, t, sumsq, junk)
                a.wait_ge(sumsq, t + 1)
                root(0, t, rms_ready)

            for c in range(3):
                a.dma_start(bgu[32 * c:32 * c + 32, :], b_gate_up[0]).then_inc(bgu_in, 16)
            a.dma_start(wrt[:], w_router[0].rearrange("(k p) e -> p k e", p=P)).then_inc(router_in, 16)
            a.dma_start(brt[:], b_router[0].rearrange("(e a) -> e a", a=1)).then_inc(router_in, 16)

            def take_v(h):
                for t in range(TT):
                    a.wait_ge(tiles_done, tile_done("v", 2 * h + t))
                    if h >= 2:
                        a.wait_ge(jobs_done, job_done("o", 2 * (h - 2) + 1))
                    nc.scalar.copy(v[:, h % 2, t, :], tile_bank(TILE["v", 2 * h + t])[:]).then_inc(v_ready, 1)

            def square_o(h):
                for b in range(2):
                    a.wait_ge(jobs_done, job_done("o", 2 * h + b))
                    if h >= 1:
                        a.wait_ge(jobs_done, job_done("ss", h - 1))
                    nc.scalar.activation(osq[:, b, :, :], job_bank("o", 2 * h + b)[:].rearrange(
                        "p (a t) -> p a t", a=2), ACT.Square).then_inc(osq_ready, 1)

            def root_o(h):
                a.wait_ge(jobs_done, job_done("ss", h))
                if h >= 1:
                    a.wait_ge(gated_o, h)
                nc.scalar.activation(rr, job_bank("ss", h)[:, 0:S], ACT.Sqrt, bias=eps_t[:, 0:1],
                                     scale=1.0 / DV).then_inc(orms_ready, 1)

            def split_hi(n):
                a.wait_ge(loaded[n % 2], 16 * (n // 2 + 1))
                if n >= 2:
                    a.wait_ge(tiles_done, chunk_done(n - 2))
                for src, dst in zip(chunk_halves(n, ring[:, n % 2, :]), chunk_halves(n, w_hi[n % 2][:])):
                    nc.scalar.copy(dst, src).then_inc(hi_ready, 1)

            def take_pool(g):
                a.wait_ge(tiles_done, tile_done("pool", g))
                a.wait_ge(pool_step, 7)
                if g >= 2:
                    a.wait_ge(pooled_ready, g - 1)
                nc.scalar.copy(pu[:, g % 2, :, PAD:], tile_bank(TILE["pool", g])[:].rearrange(
                    "p (a t) -> p a t", a=2)).then_inc(pu_ready, 1)

            def scale_ypool(g):
                a.wait_ge(jobs_done, job_done("ypool", g))
                for c in range(2):
                    n = 2 * g + c
                    nc.scalar.activation(m[:, n, :], job_bank("ypool", g)[:, S * c:S * c + S], ACT.Copy,
                                         scale=vec[:, 1, n:n + 1]).then_inc(ypool_ready, 1)

            def gate_a(j):
                a.wait_ge(tiles_done, tile_done("ga", j))
                if j >= 2:
                    a.wait_ge(ga_used, j - 1)
                else:
                    a.wait_ge(gated_o, HEADS + 7 + j)
                nc.scalar.activation(tmp[:, j % 2, :], tile_bank(TILE["ga", j])[:], ACT.Sigmoid
                                     ).then_inc(ga_ready, 1)

            def gate_b(j):
                a.wait_ge(tiles_done, tile_done("gb", j))
                a.wait_ge(jobs_done, job_done("ypool", 3))
                nc.scalar.activation(sigB[:, 2 * j:2 * j + 2, :], tile_bank(TILE["gb", j])[:].rearrange(
                    "p (a t) -> p a t", a=2), ACT.Sigmoid).then_inc(gb_ready, 1)

            def gate_r(j):
                a.wait_ge(tiles_done, tile_done("gr", j))
                if j >= 2:
                    a.wait_ge(gated_o, HEADS + j - 1)
                nc.scalar.activation(tmp[:, j % 2, :], tile_bank(TILE["gr", j])[:], ACT.Sigmoid
                                     ).then_inc(gr_ready, 1)

            split_hi(0)
            a.wait_ge(vec_ready, 1)
            for n, (kind, j) in enumerate(CHUNKS):
                if n + 1 < N1:
                    split_hi(n + 1)
                if kind == "v":
                    take_v(j)
                    if j >= 2:
                        root_o(j - 2)
                    if j >= 1:
                        square_o(j - 1)
                elif kind == "pool":
                    take_pool(2 * j)
                    take_pool(2 * j + 1)
                    root_o(2 + j)
                    if j == 0:
                        square_o(3)
                elif kind == "gr":
                    gate_r(2 * j)
                    gate_r(2 * j + 1)
                elif kind == "ga":
                    gate_a(2 * j)
                    gate_a(2 * j + 1)
                    scale_ypool(2 * j)
                    scale_ypool(2 * j + 1)
                elif kind == "gb":
                    gate_b(2 * j)
                    gate_b(2 * j + 1)

            a.wait_ge(merged, 4)
            load_table(ACT.Sqrt)
            a.dma_start(bdown, b_down[0]).then_inc(bdown_in, 16)
            a.dma_start(gfin, g_final.rearrange("(a d) -> a d", a=1).to_broadcast([P, D])).then_inc(gfin_in, 16)

            def take_part(c, t):
                if c == 0:
                    a.wait_ge(xn_ready, t + 1)
                else:
                    a.wait_ge(resid_ready, 2 * (c - 1) + t + 1)
                nc.scalar.copy(parts[:, c, t, :], xn[:, t, :] if c == 0 else resid[:, t, :]).then_inc(part_ready, 1)

            def take_logits(t):
                a.wait_ge(jobs_done, job_done("logits", t))
                nc.scalar.activation(LT[:, P * t:P * t + P], job_bank("logits", t)[0:NE, 0:P], ACT.Identity,
                                     bias=brt[:, 0:1]).then_inc(LT_ready, 1)

            for t in range(TT):
                a.wait_ge(x1_ready, 3 + t)
                square(xs[:, t, :], 2, t, sumsq2, junk)
                a.wait_ge(sumsq2, t + 1)
                root(2, t, rms2_ready)
                take_part(0, t)
            load_table(ACT.Exp)
            a.wait_ge(router_in, 32)
            take_logits(0)
            take_part(1, 0)
            take_logits(1)
            take_part(1, 1)
            take_part(2, 0)
            take_part(2, 1)
            for t in range(TT):
                a.wait_ge(top_ready, t + 1)
                nc.scalar.activation(Eg[:, t, :], L[:, t, :], ACT.Exp, bias=stat[:, 4, t:t + 1]
                                     ).then_inc(exp_ready, 1)
            load_table(ACT.Sigmoid)
            a.wait_ge(jobs_done, job_done("gT"))
            nc.scalar.copy(GT, job_bank("gT")[0:NE, 0:S]).then_inc(GT_ready, 1)

            a.wait_ge(items_ready, 1)
            end = a.value_load(nitems[0:1, 0:1], min_val=NE, max_val=NE * MAX_BLOCKS)
            with a.Fori(0, end) as i:
                a.wait_ge(g7_ready, i + 1)
                nc.scalar.activation(gs, g7, ACT.Sigmoid, scale=ALPHA).then_inc(sig_ready, 1)
                a.wait_ge(CT_done, i + 1)
                nc.scalar.copy(CT, bank[3][:, 0:S].rearrange("p (t s) -> p t s", t=TT)).then_inc(CT_ready, 1)
                a.wait_ge(aT_done, i + 1)
                nc.scalar.copy(aT, bank[0][:].rearrange("p (j h s) -> p j h s", j=4, h=2)).then_inc(aT_ready, 1)
                a.wait_ge(down_done, i + 1)
                nc.scalar.copy(y, bank[3][:]).then_inc(y_ready, 1)

            load_table(ACT.Sqrt)
            for t in range(TT):
                a.wait_ge(x2_ready, 2 * t + 2)
                square(xs[:, t, :], 5, t, sumsq3, late_junk)
                a.wait_ge(sumsq3, t + 1)
                root(5, t, rms3_ready)
            for n in range(4):
                a.wait_ge(pw_done, n + 1)
                nc.scalar.copy(pw[:, n // 2, HALF * (n % 2):HALF * (n % 2) + HALF], bank[n][:]).then_inc(pw_ready, 1)
            load_table(ACT.Sigmoid)
            for n in range(4):
                a.wait_ge(gate_done, n + 1)
                nc.scalar.activation(tmp[:, n % 2, :] if n < 2 else sigB[:, 2 * n - 4:2 * n - 2, :].rearrange(
                    "p a t -> p (a t)"), bank[n][:], ACT.Sigmoid).then_inc(gate_ready, 1)
                if n == 2:
                    a.wait_ge(x3_ready, 2)
                    square(xs[:, 0, :], 8, 0, sumsq4, late_junk)
            load_table(ACT.Sqrt)
            a.wait_ge(sumsq4, 1)
            root(8, 0, rms4_ready)
            a.wait_ge(x3_ready, 4)
            square(xs[:, 1, :], 8, 1, sumsq4, late_junk)
            a.wait_ge(sumsq4, 2)
            root(8, 1, rms4_ready)

        @block.vector
        def _(dve):
            steps = [0]

            def link(ins):
                steps[0] += 1
                ins.then_inc(dve_step, 1)
                dve.wait_ge(dve_step, steps[0])

            def one_hot(e, b):
                for t in range(TT):
                    ins = nc.vector.tensor_scalar(hot[:, t, :], slots_io[:, bass.ds(b, 1), 0, :].rearrange(
                        "p a s -> p (a s)"), pos[:, t, bass.ds(e, 1)], None, ALU.is_equal)
                    ins.then_inc(hot_ready, 1)

            def bias_pick(e):
                nc.vector.tensor_scalar(bsel[0:96, :], ones[0:96, 0:CAP], pick[:, bass.ds(e, 1)], None,
                                        ALU.mult).then_inc(bsel_ready, 1)

            def take_gathered():
                nc.vector.tensor_tensor(XT, bank[2][:].rearrange("p (k s) -> p k s", k=KT),
                                        vec[:, 2, :].unsqueeze(2).to_broadcast([P, KT, CAP]),
                                        ALU.mult).then_inc(XT_ready, 1)

            dve.wait_ge(jobs_done, job_done("vec"))
            nc.vector.tensor_copy(vec[:], job_bank("vec")[:, 0:32].rearrange("p (n k) -> p n k", n=4)
                                  ).then_inc(vec_ready, 1)

            def normalise(row, t, rms, ready):
                dve.wait_ge(rms, t + 1)
                link(nc.vector.reciprocal(stat[:, row, t:t + 1], stat[:, row, t:t + 1]))
                nc.vector.tensor_scalar(xn[:, t, :], xs[:, t, :], stat[:, row, t:t + 1], None,
                                        ALU.mult).then_inc(ready, 1)

            def scaled(out, src, g, c):
                return nc.vector.tensor_tensor(out, src[:].rearrange("p (k s) -> p k s", k=4),
                                               vec[:, g, 4 * c:4 * c + 4].unsqueeze(2).to_broadcast([P, 4, P]),
                                               ALU.mult)

            for t in range(TT):
                normalise(1, t, rms_ready, xs_ready)
            dve.wait_ge(vec_ready, 1)
            for j in range(4):
                t, c = j // 2, j % 2
                to = (slice(None), slice(4 * c, 4 * c + 4), slice(P * t, P * t + P))
                h32 = tmp[:, j % 2, :].rearrange("p (k s) -> p k s", k=4)
                dve.wait_ge(jobs_done, job_done("xT", j))
                link(scaled(h32, job_bank("xT", j), 0, c))
                link(nc.vector.tensor_copy(h_hi[to], h32))
                nc.vector.tensor_tensor(h_lo[to], h32, h_hi[to].bitcast(F32), ALU.subtract).then_inc(hT_ready, 1)
                dve.wait_ge(hT_ready, j + 1)

            def split_lo(n):
                for b, (raw, hi, lo) in enumerate(zip(chunk_halves(n, ring[:, n % 2, :]),
                                                      chunk_halves(n, w_hi[n % 2][:]),
                                                      chunk_halves(n, w_lo[n % 2][:]))):
                    dve.wait_ge(hi_ready, 2 * n + b + 1)
                    nc.vector.tensor_tensor(lo, raw, hi.bitcast(F32), ALU.subtract).then_inc(lo_ready, 1)

            def rotate(kind, h, dst, ready):
                n = TILE[kind, h]
                dve.wait_ge(tiles_done, n + 1)
                if h >= 2:
                    dve.wait_ge(jobs_done, job_done("scores", h - 2))
                src = tile_bank(n)[:].rearrange("p (a t) -> p a t", a=2)
                for c in range(2):
                    ins = nc.vector.tensor_tensor(tmp[:, c, :].rearrange("p (a t) -> p a t", a=2), src,
                                                  rot[:, c:c + 1, :].to_broadcast([P, 2, S]), ALU.mult)
                    link(ins)
                nc.vector.tensor_tensor(dst[:, h % 2, 0, :], tmp[:, 0, 0:S], tmp[:, 1, S:2 * S],
                                        ALU.subtract).then_inc(ready, 1)
                nc.vector.tensor_tensor(dst[:, h % 2, 1, :], tmp[:, 0, S:2 * S], tmp[:, 1, 0:S],
                                        ALU.add).then_inc(ready, 1)
                dve.wait_ge(ready, 2 * h + 2)

            def mask_scores(h):
                dve.wait_ge(jobs_done, job_done("scores", h))
                nc.vector.tensor_tensor(sT[:, h, :], job_bank("scores", h)[:, 0:384], dec[:, h, :],
                                        ALU.mult).then_inc(sT_ready, 1)

            def split_biases():
                dve.wait_ge(bgu_in, 48)
                link(nc.vector.tensor_copy(bias_parts[:], bgu))
                link(nc.vector.tensor_tensor(bgu, bgu, bias_parts[:], ALU.subtract))
                nc.vector.tensor_copy(bias_parts[32:64, :], bgu[32:64, :]).then_inc(bias_ready, 1)
                link(nc.vector.tensor_copy(bias_parts[64:96, :], bgu[64:96, :]))
                link(nc.vector.tensor_tensor(bgu[64:96, :], bgu[64:96, :], bias_parts[64:96, :], ALU.subtract))
                nc.vector.tensor_copy(bias_parts[64:96, :], bgu[64:96, :]).then_inc(bias_ready, 1)

            def copy_o(h):
                for b in range(2):
                    dve.wait_ge(osq_ready, 2 * h + b + 1)
                    c = 4 * h + 2 * b
                    nc.vector.tensor_copy(oT[:, c:c + 2, :], job_bank("o", 2 * h + b)[:].rearrange(
                        "p (a t) -> p a t", a=2)).then_inc(o_copied, 1)

            def norm_o(h):
                dve.wait_ge(orms_ready, h + 1)
                link(nc.vector.reciprocal(rr, rr))
                dve.wait_ge(o_copied, 2 * h + 2)
                nc.vector.tensor_tensor(oT[:, 4 * h:4 * h + 4, :], oT[:, 4 * h:4 * h + 4, :],
                                        rr.unsqueeze(1).to_broadcast([P, 4, S]), ALU.mult).then_inc(gated_o, 1)

            def gate_o(j):
                dve.wait_ge(gr_ready, j + 1)
                two = slice(2 * j, 2 * j + 2)
                g = tmp[:, j % 2, :].rearrange("p (a t) -> p a t", a=2)
                link(nc.vector.tensor_tensor(tmp[:, j % 2, :], tile_bank(TILE["gr", j])[:], tmp[:, j % 2, :],
                                             ALU.mult))
                link(nc.vector.tensor_tensor(g, oT[:, two, :], g, ALU.mult))
                link(nc.vector.tensor_copy(o_hi[:, two, :], g))
                nc.vector.tensor_tensor(o_lo[:, two, :], g, o_hi[:, two, :].bitcast(F32),
                                        ALU.subtract).then_inc(gated_o, 1)

            def merge(j):
                dve.wait_ge(tiles_done, tile_done("ro", j))
                two = slice(2 * j, 2 * j + 2)
                link(nc.vector.tensor_tensor(sigB[:, two, :], tile_bank(TILE["ro", j])[:].rearrange(
                    "p (a t) -> p a t", a=2), sigB[:, two, :], ALU.mult))
                link(nc.vector.tensor_tensor(sigB[:, two, :], m[:, two, :], sigB[:, two, :], ALU.add))
                link(nc.vector.tensor_copy(h_hi[:, two, :], sigB[:, two, :]))
                nc.vector.tensor_tensor(h_lo[:, two, :], sigB[:, two, :], h_hi[:, two, :].bitcast(F32),
                                        ALU.subtract).then_inc(merged, 1)

            def add_residual(n):
                dve.wait_ge(tiles_done, tile_done("wo", n))
                cols = slice(HALF * (n // 2), HALF * (n // 2) + HALF)
                nc.vector.tensor_tensor(xs[:, n % 2, cols], xs[:, n % 2, cols], tile_bank(TILE["wo", n])[:],
                                        ALU.add).then_inc(x1_ready, 1)

            split_lo(0)
            for n, (kind, j) in enumerate(CHUNKS):
                if n + 1 < N1:
                    split_lo(n + 1)
                if kind in "qk":
                    if n == 0:
                        dve.wait_ge(rot_in, 16)
                    for h in (2 * j, 2 * j + 1):
                        rotate(kind, h, qr if kind == "q" else kr, q_ready if kind == "q" else k_ready)
                    if (kind, j) == ("k", 0):
                        dve.wait_ge(jobs_done, job_done("pT"))
                        nc.vector.tensor_copy(pT[:], job_bank("pT")[:].rearrange("p (a t) -> p a t", a=2)
                                              ).then_inc(pT_ready, 1)
                    if (kind, j) == ("q", 1):
                        dve.wait_ge(dec_in, 16)
                        mask_scores(0)
                        mask_scores(1)
                elif kind == "v":
                    if j == 0:
                        mask_scores(2)
                        mask_scores(3)
                        split_biases()
                    if j >= 2:
                        norm_o(j - 2)
                    if j >= 1:
                        copy_o(j - 1)
                elif kind == "pool":
                    norm_o(2 + j)
                    if j == 0:
                        copy_o(3)
                elif kind == "gr":
                    if j == 0:
                        dve.wait_ge(gated_o, HEADS)
                    gate_o(2 * j)
                    gate_o(2 * j + 1)
                elif kind == "ro":
                    if j == 0:
                        dve.wait_ge(gb_ready, 4)
                        dve.wait_ge(ga_used, 4)
                        dve.wait_ge(tables, 11)
                        nc.vector.memset(y, 0.0).then_inc(y_ready, 1)
                        nc.vector.memset(CT, 0.0).then_inc(CT_ready, 1)
                        bias_pick(0)
                    merge(j)
                elif kind == "wo":
                    if j == 0:
                        add_residual(0)
                        add_residual(1)

            add_residual(2)
            normalise(3, 0, rms2_ready, xn_ready)
            add_residual(3)
            for t in range(TT):
                if t == 1:
                    normalise(3, 1, rms2_ready, xn_ready)
                for c in range(2):
                    dve.wait_ge(jobs_done, job_done("hT", 2 * t + c))
                    scaled(h2T[:, 4 * c:4 * c + 4, P * t:P * t + P], job_bank("hT", 2 * t + c), 2, c
                           ).then_inc(h2T_ready, 1)

            for t in range(TT):
                dve.wait_ge(jobs_done, job_done("logitsT", t))
                link(nc.vector.tensor_copy(L[:, t, :], job_bank("logitsT", t)[:, 0:NE]))
                link(nc.vector.max(top[:, t, :], L[:, t, :]))
                nc.vector.tensor_scalar(stat[:, 4, t:t + 1], top[:, t, 0:1], -1.0, None,
                                        ALU.mult).then_inc(top_ready, 1)
                link(nc.vector.max_index(topi[:, t, :], top[:, t, :], L[:, t, :]))
                link(nc.vector.tensor_copy(topf[:, t, :], topi[:, t, :]))
                link(nc.vector.tensor_scalar(Msel[:, t, :], exp_io[:], topf[:, t, 0:1], None, ALU.is_equal))
                for k in range(1, TOPK):
                    link(nc.vector.scalar_tensor_tensor(out=Msel[:, t, :], in0=exp_io[:],
                                                        scalar=topf[:, t, k:k + 1], in1=Msel[:, t, :],
                                                        op0=ALU.is_equal, op1=ALU.add))
                nc.vector.tensor_copy(Mb[:, t, :], Msel[:, t, :]).then_inc(Mb_ready, 1)
            dve.wait_ge(exp_ready, TT)
            link(nc.vector.tensor_tensor(Eg[:], Eg[:], Msel[:], ALU.mult))
            link(nc.vector.reduce_sum(stat[:, 7, :], Eg[:], AX_X))
            link(nc.vector.reciprocal(stat[:, 7, :], stat[:, 7, :]))
            for t in range(TT):
                nc.vector.tensor_scalar(G[:, t, :], Eg[:, t, :], stat[:, 7, t:t + 1], None,
                                        ALU.mult).then_inc(G_ready, 1)
            dve.wait_ge(jobs_done, job_done("rank"))
            rank = job_bank("rank")[:, 0:2 * NE].rearrange("p (t e) -> p t e", t=TT)
            link(nc.vector.scalar_tensor_tensor(out=pos[:], in0=rank, scalar=1.0, in1=Msel[:],
                                                op0=ALU.add, op1=ALU.mult))
            link(nc.vector.tensor_scalar(pos[:], pos[:], -1.0, None, ALU.add))
            one_hot(0, 0)
            link(nc.vector.reduce_max(nit[:, 0:1], job_bank("rank")[0:1, 2 * NE:3 * NE], AX_X))
            link(nc.vector.tensor_scalar(nit[:, 2:2 + MAX_BLOCKS], steps64[:], nit[:, 0:1], float(NE),
                                         ALU.is_lt, ALU.mult))
            link(nc.vector.reduce_sum(nit[:, 1:2], nit[:, 2:2 + MAX_BLOCKS], AX_X))
            nc.vector.tensor_copy(nitems[:], nit[:, 1:2]).then_inc(items_ready, 1)

            dve.wait_ge(gathered, 1)
            take_gathered()
            dve.wait_ge(items_ready, 1)
            end = dve.value_load(nitems[0:1, 0:1], min_val=NE, max_val=NE * MAX_BLOCKS)
            with dve.Fori(0, end) as i:
                e, b = i & (NE - 1), i >> 5
                nxt = i + 1
                dve.wait_ge(CT_done, i)
                for t in range(TT):
                    nc.vector.tensor_scalar(Cg[:, t, :], slots_io[:, bass.ds(b, 1), :, :].rearrange(
                        "p a h s -> p (a h s)"), pos[:, t, bass.ds(e, 1)], G[:, t, bass.ds(e, 1)],
                        ALU.is_equal, ALU.mult).then_inc(Cg_ready, 1)
                dve.wait_ge(gathered, i + 1)
                one_hot(nxt & (NE - 1), nxt >> 5)
                dve.wait_ge(glu_done, i + 1)
                nc.vector.tensor_scalar(g7, bank[0][:], LIMIT, None, ALU.min).then_inc(g7_ready, 1)
                dve.wait_ge(sig_ready, i + 1)
                nc.vector.tensor_tensor(gs, g7, gs, ALU.mult).then_inc(gs_ready, 1)
                dve.wait_ge(lin_done, i + 1)
                nc.vector.tensor_scalar(l7, bank[1][:], LIMIT, -LIMIT, ALU.min, ALU.max).then_inc(l7_ready, 1)
                dve.wait_ge(gs_ready, i + 1)
                dve.wait_ge(l7_ready, i + 1)
                nc.vector.scalar_tensor_tensor(out=act, in0=l7, scalar=1.0, in1=gs, op0=ALU.add,
                                               op1=ALU.mult).then_inc(act_ready, 1)
                bias_pick(nxt & (NE - 1))
                dve.wait_ge(gathered, i + 2)
                take_gathered()

            for n in range(4):
                dve.wait_ge(moe_done, n + 1)
                cols = slice(HALF * (n % 2), HALF * (n % 2) + HALF)
                nc.vector.tensor_tensor(xs[:, n // 2, cols], xs[:, n // 2, cols], bank[4 + n][:],
                                        ALU.add).then_inc(x2_ready, 1)
            for t in range(TT):
                normalise(6, t, rms3_ready, u_ready)
            for n in range(4):
                t, c = n // 2, n % 2
                dve.wait_ge(uT_done, n + 1)
                scaled(uT[:, 4 * c:4 * c + 4, P * t:P * t + P], bank[4 + n], 3, c).then_inc(uT_ready, 1)
            dve.wait_ge(pw_ready, 4)
            for n in range(4):
                t = n // 2
                cols = slice(HALF * (n % 2), HALF * (n % 2) + HALF)
                dve.wait_ge(gate_ready, n + 1)
                src = tmp[:, n % 2, :] if n < 2 else sigB[:, 2 * n - 4:2 * n - 2, :].rearrange("p a t -> p (a t)")
                link(nc.vector.tensor_tensor(pw[:, t, cols], pw[:, t, cols], src, ALU.mult))
                nc.vector.tensor_tensor(xs[:, t, cols], xs[:, t, cols], pw[:, t, cols],
                                        ALU.add).then_inc(x3_ready, 1)
            dve.wait_ge(gfin_in, 16)
            for t in range(TT):
                dve.wait_ge(rms4_ready, t + 1)
                link(nc.vector.reciprocal(stat[:, 9, t:t + 1], stat[:, 9, t:t + 1]))
                nc.vector.scalar_tensor_tensor(out=oT[:, 8 + 4 * t:12 + 4 * t, :].rearrange("p c s -> p (c s)"),
                                               in0=xs[:, t, :], scalar=stat[:, 9, t:t + 1], in1=gfin,
                                               op0=ALU.mult, op1=ALU.mult).then_inc(out_ready, 1)

        @block.tensor
        def _(pe):
            def take_job(kind, j=0):
                n = JOB[kind, j]
                if n >= 4:
                    wait_job_free(pe, n - 4)
                return bank[4 + n % 4]

            def transposes(kind, t, src):
                for c in range(2):
                    dst = take_job(kind, 2 * t + c)
                    for k in range(4):
                        col = P * (4 * c + k)
                        last = nc.tensor.transpose(dst[:, P * k:P * k + P], src[:, t, col:col + P], ident[:])
                    last.then_inc(jobs_done, 1)

            pe.wait_ge(tables, 4)
            pe.wait_ge(vec_in, 64)
            nc.tensor.transpose(take_job("vec")[:, 0:32], vrow[:], ident[0:32, 0:32]).then_inc(jobs_done, 1)
            for t in range(TT):
                pe.wait_ge(xs_ready, t + 1)
                transposes("xT", t, xn)

            def transpose_embeddings():
                pe.wait_ge(p_in, 16)
                dst = take_job("pT")
                pr = prow.rearrange("p (t c) s -> p t (c s)", t=TT)
                for c in range(2):
                    for t in range(TT):
                        last = nc.tensor.transpose(dst[:, S * c + P * t:S * c + P * t + P],
                                                   pr[:, t, P * c:P * c + P], ident[:])
                last.then_inc(jobs_done, 1)

            def product(dst, stationary, moving, k, kts):
                (s_hi, s_lo), (m_hi, m_lo) = stationary, moving
                nc.tensor.matmul(dst, s_hi, m_hi, start=(k == 0), stop=False)
                nc.tensor.matmul(dst, s_hi, m_lo, start=False, stop=False)
                return nc.tensor.matmul(dst, s_lo, m_hi, start=False, stop=(k == kts - 1))

            def chunk(n):
                kind, j = CHUNKS[n]
                kts = 16 if kind == "ro" else KT
                w = [x[n % 2][:].rearrange("p (k n) -> p k n", k=kts) for x in (w_hi, w_lo)]
                src = (o_hi, o_lo) if kind == "ro" else (h_hi, h_lo)
                for b in range(1 if kind == "ro" else 2):
                    t = TILE[kind, j if kind == "ro" else 2 * j + b]
                    pe.wait_ge(lo_ready, 2 * n + 2 if kind in ("v", "ro", "wo") else 2 * n + b + 1)
                    if t >= 4:
                        wait_tile_free(pe, t - 4)
                    dst = tile_bank(t)
                    if kind in ("v", "wo"):
                        for k in range(kts):
                            if kind == "wo" and k % 2 == 0:
                                pe.wait_ge(merged, k // 2 + 1)
                            last = product(dst[:], [x[:, k, P * b:P * b + P] for x in src],
                                           [x[:, k, :] for x in w], k, kts)
                    else:
                        for c in range(2):
                            col = P * (2 * b + c)
                            for k in range(kts):
                                last = product(dst[:, S * c:S * c + S], [x[:, k, col:col + P] for x in w],
                                               [x[:, k, :] for x in src], k, kts)
                    last.then_inc(tiles_done, 1)

            def scores(h):
                pe.wait_ge(q_ready, 2 * h + 2)
                pe.wait_ge(k_ready, 2 * h + 2)
                dst = take_job("scores", h)
                for a in range(2):
                    nc.tensor.matmul(dst[:, 0:S], kr[:, h % 2, a, 0:P], qr[:, h % 2, a, :],
                                     start=(a == 0), stop=(a == 1))
                for a in range(2):
                    last = nc.tensor.matmul(dst[:, S:S + P], kr[:, h % 2, a, P:S], qr[:, h % 2, a, P:S],
                                            start=(a == 0), stop=(a == 1))
                last.then_inc(jobs_done, 1)

            def outputs(h):
                pe.wait_ge(sT_ready, h + 1)
                pe.wait_ge(v_ready, 2 * h + 2)
                for b in range(2):
                    dst = take_job("o", 2 * h + b)
                    for c in range(2):
                        col = P * (2 * b + c)
                        nc.tensor.matmul(dst[:, S * c:S * c + S], v[:, h % 2, 0, col:col + P], sT[:, h, 0:S],
                                         start=True, stop=False)
                        last = nc.tensor.matmul(dst[:, S * c + P:S * c + S], v[:, h % 2, 1, col:col + P],
                                                sT[:, h, S:S + P], start=False, stop=True)
                    last.then_inc(jobs_done, 1)

            def sum_squares(h):
                pe.wait_ge(osq_ready, 2 * h + 2)
                dst = take_job("ss", h)
                for n in range(4):
                    last = nc.tensor.matmul(dst[:, 0:S], ones[:], osq[:, n // 2, n % 2, :],
                                            start=(n == 0), stop=(n == 3))
                last.then_inc(jobs_done, 1)

            def pool_project(g):
                pe.wait_ge(pooled_ready, g + 1)
                pe.wait_ge(wpool_in, 16)
                dst = take_job("ypool", g)
                for c in range(2):
                    for k in range(2):
                        last = nc.tensor.matmul(dst[:, S * c:S * c + S], wpool[:, g, k, P * c:P * c + P],
                                                m[:, 2 * g + k, :], start=(k == 0), stop=(k == 1))
                last.then_inc(jobs_done, 1)

            pe.wait_ge(hT_ready, 4)
            for n, (kind, j) in enumerate(CHUNKS):
                if (kind, j) == ("ro", 0):
                    pe.wait_ge(gated_o, HEADS + 8)
                chunk(n)
                if (kind, j) == ("q", 0):
                    transpose_embeddings()
                elif (kind, j) == ("q", 1):
                    scores(0)
                    scores(1)
                elif (kind, j) == ("v", 0):
                    scores(2)
                    scores(3)
                elif kind == "v":
                    if j >= 2:
                        sum_squares(j - 2)
                    outputs(j - 1)
                elif kind == "pool":
                    sum_squares(2 + j)
                    if j == 0:
                        outputs(3)
                elif kind == "ga":
                    pool_project(2 * j)
                    pool_project(2 * j + 1)

            pe.wait_ge(router_in, 32)
            for t in range(TT):
                pe.wait_ge(xn_ready, t + 1)
                transposes("hT", t, xn)
                dst = take_job("logits", t)
                for k in range(KT):
                    if k % 4 == 0:
                        pe.wait_ge(h2T_ready, 2 * t + k // 4 + 1)
                    last = nc.tensor.matmul(dst[0:NE, 0:P], wrt[:, k, :], h2T[:, k, P * t:P * t + P],
                                            start=(k == 0), stop=(k == KT - 1))
                last.then_inc(jobs_done, 1)
            for t in range(TT):
                pe.wait_ge(LT_ready, t + 1)
                nc.tensor.transpose(take_job("logitsT", t)[:, 0:NE], LT[:, P * t:P * t + P],
                                    ident[0:NE, 0:NE]).then_inc(jobs_done, 1)
            pe.wait_ge(Mb_ready, TT)
            pe.wait_ge(tables, 11)
            dst = take_job("rank")
            for n, terms in enumerate((((before, 0),), ((onesb, 0), (before, 1)), ((onesb, 0), (onesb, 1)))):
                for k, (mat, t) in enumerate(terms):
                    last = nc.tensor.matmul(dst[:, NE * n:NE * n + NE], mat[:], Mb[:, t, :],
                                            start=(k == 0), stop=(k == len(terms) - 1))
            last.then_inc(jobs_done, 1)
            pe.wait_ge(G_ready, TT)
            dst = take_job("gT")
            for t in range(TT):
                last = nc.tensor.transpose(dst[0:NE, P * t:P * t + P], G[:, t, :], ident[:])
            last.then_inc(jobs_done, 1)

            def gather():
                for k in range(KT):
                    for c in range(3):
                        for t in range(TT):
                            last = nc.tensor.matmul(bank[2][:, CAP * k:CAP * k + CAP],
                                                    parts[:, c, t, P * k:P * k + P], hot[:, t, :],
                                                    start=(c == 0 and t == 0), stop=(c == 2 and t == TT - 1))
                last.then_inc(gathered, 1)

            def combine(final):
                for t in range(TT):
                    for h in range(2):
                        last = nc.tensor.matmul(bank[4 + 2 * t + h][:], CT[CAP * h:CAP * h + CAP, t, :],
                                                y[CAP * h:CAP * h + CAP, :], start=False, stop=final,
                                                skip_group_check=True)
                        if final:
                            last.then_inc(moe_done, 1)

            pe.wait_ge(bdown_in, 16)
            pe.wait_ge(GT_ready, 1)
            pe.wait_ge(items_ready, 1)
            for t in range(TT):
                for h in range(2):
                    nc.tensor.matmul(bank[4 + 2 * t + h][:], GT[:, P * t:P * t + P],
                                     bdown[:, HALF * h:HALF * h + HALF], start=True, stop=False,
                                     skip_group_check=True)
            pe.wait_ge(part_ready, 3 * TT)
            pe.wait_ge(hot_ready, TT)
            gather()
            pe.wait_ge(bias_ready, 2)
            end = pe.value_load(nitems[0:1, 0:1], min_val=NE, max_val=NE * MAX_BLOCKS)
            with pe.Fori(0, end) as i:
                def up(first, dst):
                    for h in range(2):
                        nc.tensor.matmul(dst[CAP * h:CAP * h + CAP, :], bsel[0:96, :],
                                         bias_parts[:, FF * (first // 2) + HALF * h:FF * (first // 2) + HALF * (h + 1)],
                                         start=True, stop=False)
                    for c in range(2):
                        n = first + c
                        w = ring[:, n, :].rearrange("p (k n) -> p k n", k=4)
                        pe.wait_ge(loaded[n], 16 * (item_loads(n) + 1) + 16 * i)
                        for k in range(4):
                            for h in range(2):
                                last = nc.tensor.matmul(dst[CAP * h:CAP * h + CAP, :], XT[:, 4 * c + k, :],
                                                        w[:, k, HALF * h:HALF * h + HALF],
                                                        start=False, stop=(c == 1 and k == 3))
                        last.then_inc(slot_used[n], 1)

                pe.wait_ge(XT_ready, i + 1)
                pe.wait_ge(bsel_ready, i + 1)
                up(0, bank[0])
                pe.wait_ge(y_ready, i + 1)
                pe.wait_ge(CT_ready, i + 1)
                combine(False)
                up(2, bank[1])
                pe.wait_ge(Cg_ready, 2 * i + 2)
                for t in range(TT):
                    last = nc.tensor.transpose(bank[3][:, P * t:P * t + P], Cg[:, t, :], ident[:])
                last.then_inc(CT_done, 1)
                pe.wait_ge(hot_ready, 2 * i + 4)
                gather()
                pe.wait_ge(act_ready, i + 1)
                for j in range(4):
                    last = nc.tensor.transpose(bank[0][:, P * j:P * j + P], act[:, P * j:P * j + P], ident[:])
                last.then_inc(aT_done, 1)
                pe.wait_ge(aT_ready, i + 1)
                pe.wait_ge(CT_ready, i + 2)
                for c in range(2):
                    n = 4 + c
                    w = ring[:, n, :].rearrange("p (k n) -> p k n", k=4)
                    pe.wait_ge(loaded[n], 16 * (item_loads(n) + 1) + 16 * i)
                    for k in range(4):
                        for h in range(2):
                            last = nc.tensor.matmul(bank[3][CAP * h:CAP * h + CAP, :], aT[:, k, c, :],
                                                    w[:, k, HALF * h:HALF * h + HALF],
                                                    start=(c == 0 and k == 0), stop=(c == 1 and k == 3))
                    last.then_inc(slot_used[n], 1)
            pe.wait_ge(y_ready, end + 1)
            combine(True)

            pe.wait_ge(XT_ready, end + 1)
            pe.wait_ge(pT_ready, 1)
            pe.wait_ge(loaded[0], 16 * (item_loads(0) + 1) + 16 * end)
            w = ring[:, 0, 0:2048].rearrange("p (k n) -> p k n", k=2)
            for n in range(4):
                t, h = n // 2, n % 2
                for k in range(2):
                    last = nc.tensor.matmul(bank[n][:], pT[:, k, P * t:P * t + P], w[:, k, HALF * h:HALF * h + HALF],
                                            start=(k == 0), stop=(k == 1))
                last.then_inc(pw_done, 1)
            for n in range(4):
                t, c = n // 2, n % 2
                pe.wait_ge(x2_ready, n + 1)
                pe.wait_ge(u_ready, t + 1)
                for k in range(4):
                    col = P * (4 * c + k)
                    last = nc.tensor.transpose(bank[4 + n][:, P * k:P * k + P], xn[:, t, col:col + P], ident[:])
                last.then_inc(uT_done, 1)
            for n in range(4):
                t, h = n // 2, n % 2
                pe.wait_ge(uT_ready, 2 * t + 2)
                pe.wait_ge(pw_ready, n + 1)
                pe.wait_ge(loaded[1 + h], 16 * (item_loads(1 + h) + 1) + 16 * end)
                w = ring[:, 1 + h, :].rearrange("p (k n) -> p k n", k=KT)
                for k in range(KT):
                    last = nc.tensor.matmul(bank[n][:], uT[:, k, P * t:P * t + P], w[:, k, :],
                                            start=(k == 0), stop=(k == KT - 1))
                last.then_inc(gate_done, 1)


def constants():
    half = D // HEADS // 2
    inv = np.power(np.float32(10000.0), -np.linspace(0.0, 1.0, half, dtype=np.float32)).astype(np.float32)
    ang = (inv[:, None] * np.arange(S, dtype=np.float32)[None, :]).astype(np.float64)
    rot = np.stack([np.cos(ang), np.sin(ang)], axis=1).astype(np.float32)
    tok = np.arange(S)
    gap = np.abs(tok[:, None] - tok[None, :])
    seen = tok[:, None] // CHUNK <= tok[None, :] // CHUNK
    decay = np.empty((P, HEADS, S + P), np.float32)
    for h in range(HEADS):
        full = np.where(seen, np.exp(np.log(1.0 - 2.0 ** (-5.0 - h)) * gap), 0.0) * (D // HEADS) ** -0.5
        decay[:, h, :S] = full[:P]
        decay[:, h, S:] = full[P:, P:]
    count = np.stack([1.0 / np.minimum(tok[:PAD] + 1.0, w) for w in WINDOWS]).astype(np.float32)
    return {"c_rot": rot, "c_decay": decay, "c_count": np.ascontiguousarray(np.broadcast_to(count, (P, 4, PAD)))}


_INS = ["x", "p", "g_mix", "w_in", "w_pool", "pool_scale", "w_ret_o", "w_out", "g_ffn", "w_router", "b_router",
        "w_gate_up", "b_gate_up", "w_down", "b_down", "g_ple", "w_ple_gate", "w_ple", "g_final"]


def kernel(**inputs):
    import concourse.bacc as bacc
    from concourse.bass_utils import run_bass_kernel_spmd

    nc = bacc.Bacc("TRN2", target_bir_lowering=False, num_devices=1)
    arrays, args = {}, []
    values = {name: np.ascontiguousarray(inputs[name]) for name in _INS} | constants()
    for name, a in values.items():
        arrays[f"in_{name}_dram"] = a
        args.append(nc.dram_tensor(f"in_{name}_dram", a.shape, mybir.dt.from_np(a.dtype), kind="ExternalInput").ap())
    args.append(nc.dram_tensor("out_dram", (1, S, D), F32, kind="ExternalOutput").ap())
    build_kernel(nc, *args)
    r = run_bass_kernel_spmd(nc, [arrays], core_ids=[0])
    return r.results[0]["out_dram"]
```

```python
from contextlib import ExitStack

import numpy as np

import concourse.bass as bass
from concourse import mybir

F32 = mybir.dt.float32
BF16 = mybir.dt.bfloat16
F32R = mybir.dt.float32r
I32 = mybir.dt.int32
U32 = mybir.dt.uint32
ALU = mybir.AluOpType
ACT = mybir.ActivationFunctionType
AX_X = mybir.AxisListType.X

P = 128
D = 1024
S = 256
KT = D // P
TT = S // P
PLE = 256
HEADS = 4
DV = 2 * D // HEADS
NE = 32
TOPK = 4
FF = 1024
CHUNK = 64
EPS = 1e-6
ALPHA = 1.702
LIMIT = 7.0
WINDOWS = (2, 4, 8, 16)
PAD = max(WINDOWS)
HALF = 512
CAP = 64
MAX_BLOCKS = S // CAP
SLOTS = 6
SLOT = 4096

COL = {"pool": 0, "q": D, "k": 2 * D, "v": 3 * D, "gr": 5 * D, "ga": 7 * D, "gb": 8 * D}

CHUNKS = ([("q", 0), ("k", 0), ("q", 1), ("k", 1)] + [("v", h) for h in range(HEADS)]
          + [("pool", j) for j in range(2)] + [("gr", j) for j in range(4)]
          + [(k, j) for k in ("ga", "gb") for j in range(2)]
          + [("ro", j) for j in range(4)] + [("wo", j) for j in range(2)])
N1 = len(CHUNKS)
TILES = []
for _kind, _j in CHUNKS:
    TILES += [(_kind, _j)] if _kind == "ro" else [(_kind, 2 * _j), (_kind, 2 * _j + 1)]
TILE = {x: n for n, x in enumerate(TILES)}

JOBS = [("vec", 0)] + [("xT", j) for j in range(4)]
for _h in range(HEADS):
    JOBS.append(("scores", _h))
JOBS.append(("pT", 0))
for _h in range(HEADS):
    JOBS += [("o", 2 * _h), ("o", 2 * _h + 1), ("ss", _h)]
JOBS += [("ypool", g) for g in range(4)]
JOBS += [("hT", j) for j in range(4)]
JOBS += [("logits", 0), ("logits", 1), ("logitsT", 0), ("logitsT", 1), ("rank", 0)]
JOB = {x: n for n, x in enumerate(JOBS)}

PARTS = [(0, 0), (1, 0), (0, 1), (1, 1), (2, 0), (2, 1)]
PART = {x: n for n, x in enumerate(PARTS)}


def job_done(kind, j=0):
    return JOB[kind, j] + 1


def tile_done(kind, j=0):
    return TILE[kind, j] + 1


def chunk_done(n):
    kind, j = CHUNKS[n]
    return tile_done(kind, j if kind == "ro" else 2 * j + 1)


def build_kernel(nc, x, p, g_mix, w_in, w_pool, pool_scale, w_ret_o, w_out, g_ffn, w_router, b_router,
                 w_gate_up, b_gate_up, w_down, b_down, g_ple, w_ple_gate, w_ple, g_final,
                 c_rot, c_decay, c_count, out):
    x_v = x[0].rearrange("(t p) d -> p t d", p=P)
    out_v = out[0].rearrange("(t p) d -> p t d", p=P)
    p_v = p[0, 0].rearrange("(t p) d -> p t d", p=P)
    w_in_v = w_in[0].rearrange("(k p) n -> p k n", p=P)
    w_pool_v = w_pool[0].rearrange("g (c p) d -> p g c d", p=P)
    w_ro_v = w_ret_o[0].rearrange("(k p) n -> p k n", p=P)
    w_out_v = w_out[0].rearrange("(k p) n -> p k n", p=P)
    w_pg_v = w_ple_gate[0].rearrange("(k p) n -> p k n", p=P)
    w_ple_v = w_ple[0].rearrange("(k p) n -> p k n", p=P)

    with ExitStack() as ctx:
        def sb(name, shape, dt=F32):
            return ctx.enter_context(nc.sbuf_tensor(name, shape, dt))

        def sem(name):
            return ctx.enter_context(nc.semaphore(name))

        def next_address():
            return -(-nc.sbuf_base // 32) * 32

        ring_at = next_address()
        ring = sb("ring", [P, SLOTS, SLOT])

        def over(name, shape, at):
            return nc.alloc_sbuf_tensor_at(name, shape, F32R, offset=at)

        w_hi = [over(f"w_hi{b}", [P, SLOT], ring_at + 4 * SLOT * (2 + 2 * b)) for b in range(2)]
        w_lo = [over(f"w_lo{b}", [P, SLOT], ring_at + 4 * SLOT * (3 + 2 * b)) for b in range(2)]
        xs = sb("xs", [P, TT, D])
        h_at = next_address()
        h_hi = sb("h_hi", [P, KT, S], F32R)
        h_lo = sb("h_lo", [P, KT, S], F32R)
        assert nc.sbuf_base == h_at + 4 * SLOT
        odd_slot = nc.alloc_sbuf_tensor_at("odd_slot", [P, SLOT], F32, offset=h_at)
        m = sb("m", [P, KT, S])
        sigB = sb("sigB", [P, KT, S])
        o_at = next_address()
        oT = sb("oT", [P, 16, S])
        arena_at = next_address()
        arena = sb("arena", [P, 9312])
        o_hi = over("o_hi", [P, 16, S], o_at)
        o_lo = over("o_lo", [P, 16, S], arena_at)
        bias_parts = sb("bias_parts", [96, 2 * FF + D], BF16)
        wrt = sb("wrt", [P, KT, NE])
        ident = sb("ident", [P, P])
        ones = sb("ones", [P, P])
        onesb = sb("onesb", [P, P], BF16)
        before = sb("before", [P, P], BF16)
        pick = sb("pick", [96, NE])
        slots_io = sb("slots_io", [P, MAX_BLOCKS + 1, 2, CAP])
        exp_io = sb("exp_io", [P, NE])
        steps64 = sb("steps64", [1, MAX_BLOCKS])
        eps_t = sb("eps_t", [P, 1])
        vrow = sb("vrow", [32, P])
        vec = sb("vec", [P, 4, KT])
        brow = sb("brow", [P, NE])
        zero_row = sb("zero_row", [1, HALF], BF16)
        stat = sb("stat", [P, 12, TT])
        scrap = sb("scrap", [P, 1])
        L = sb("L", [P, TT, NE])
        top = sb("top", [P, TT, 8])
        topi = sb("topi", [P, TT, 8], U32)
        topf = sb("topf", [P, TT, 8])
        Msel = sb("Msel", [P, TT, NE])
        Mb = sb("Mb", [P, TT, NE], BF16)
        Eg = sb("Eg", [P, TT, NE])
        G = sb("G", [P, TT, NE])
        pos = sb("pos", [P, TT, NE])
        nit = sb("nit", [1, 8])
        nitems = sb("nitems", [1, 1], I32)

        cut = [0]

        def part(words):
            cut[0] += words
            assert cut[0] <= 9312
            return arena[:, cut[0] - words:cut[0]]

        v = part(2048).rearrange("p (b t n) -> p b t n", b=2, t=TT)
        sT = part(1536).rearrange("p (h n) -> p h n", h=HEADS)
        dec = part(1536).rearrange("p (h n) -> p h n", h=HEADS)
        rot = part(512).rearrange("p (a t) -> p a t", a=2)
        osq = part(1024).rearrange("p (b a t) -> p b a t", b=2, a=2)
        rr = part(256)
        start_rot = cut[0]
        qr = part(1024).rearrange("p (b a t) -> p b a t", b=2, a=2)
        kr = part(1024).rearrange("p (b a t) -> p b a t", b=2, a=2)
        cut[0] = start_rot
        pu = part(4 * (PAD + S)).rearrange("p (b a t) -> p b a t", b=2, a=2)
        pa = part(2 * (PAD + S)).rearrange("p (a t) -> p a t", a=2)
        pb = part(2 * (PAD + S)).rearrange("p (a t) -> p a t", a=2)
        h32 = v.rearrange("p b t n -> p (b t) n")
        pT = rot
        recip_count = sb("recip_count", [P, 4, PAD])
        cut[0] = 0
        parts = part(3072).bitcast(BF16).rearrange("p (c t d) -> p c t d", c=3, t=TT)
        resid = part(2048).rearrange("p (t d) -> p t d", t=TT)
        XT = part(512).rearrange("p (k s) -> p k s", k=KT)
        Cg = part(256).rearrange("p (t s) -> p t s", t=TT)
        CT = part(256).rearrange("p (t s) -> p t s", t=TT)
        hot = part(64).bitcast(BF16).rearrange("p (t s) -> p t s", t=TT)
        bsel = part(32).bitcast(BF16)
        w_ple_sb = arena[:, cut[0]:cut[0] + 2048].rearrange("p (k n) -> p k n", k=2)
        g7, gs, l7, act = part(512), part(512), part(512), part(512)
        aT = part(512).rearrange("p (j h s) -> p j h s", j=4, h=2)
        y = part(512)
        tmp = sb("tmp", [P, 2, 512])
        LT = tmp[0:NE, 0, 0:S]
        bgu = sigB[0:96].rearrange("p k t -> p (k t)")
        bdn = m[0:96, 4:8, :].rearrange("p k t -> p (k t)")
        wpool = sigB[:].rearrange("p (g c) d -> p g c d", g=4)
        prow = m[:, 0:2, :]
        xn = oT[:, 0:8, :].rearrange("p (t c) s -> p t (c s)", t=TT)
        junk = oT[:, 8:12, :].rearrange("p c s -> p (c s)")
        gfin = sigB[:, 4:8, :].rearrange("p k t -> p (k t)")
        late_junk = arena[:, 0:D]
        uT = arena[:, 2048:4096].rearrange("p (k t) -> p k t", k=KT)
        h2T = m
        pw = m[:, :, :].rearrange("p (t n) s -> p t (n s)", t=TT)

        bank = [ctx.enter_context(nc.psum_tensor(f"bank{i}", [P, 512], F32)) for i in range(8)]

        PW_BANKS = [bank[n] for n in (2, 0, 1, 3)]

        def tile_bank(n):
            return bank[n % 4]

        def job_bank(kind, j=0):
            return bank[4 + JOB[kind, j] % 4]

        loaded = [sem(f"loaded{i}") for i in range(SLOTS)]
        loaded_odd = sem("loaded_odd")
        x_in = [sem(f"x_in{t}") for t in range(TT)]
        wpool_in = sem("wpool_in")
        hi_ready = sem("hi_ready")
        lo_ready = sem("lo_ready")
        stats_ready = sem("stats_ready")
        warm = sem("warm")
        vec_in = sem("vec_in")
        p_in = sem("p_in")
        rot_in = sem("rot_in")
        dec_in = sem("dec_in")
        count_in = sem("count_in")
        router_in = sem("router_in")
        bgu_in = sem("bgu_in")
        bdn_in = sem("bdn_in")
        w_ple_in = sem("w_ple_in")
        gfin_in = sem("gfin_in")
        out_done = sem("out_done")
        tables = sem("tables")
        tiles_done = sem("tiles_done")
        jobs_done = sem("jobs_done")
        o_copied = sem("o_copied")
        dve_step = sem("dve_step")
        act_step = sem("act_step")
        pool_step = sem("pool_step")
        sumsq = sem("sumsq")
        rms_ready = sem("rms_ready")
        xs_ready = sem("xs_ready")
        h32_ready = sem("h32_ready")
        lo_by_pool = sem("lo_by_pool")
        h_hi_ready = sem("h_hi_ready")
        hT_ready = sem("hT_ready")
        vec_ready = sem("vec_ready")
        pT_ready = sem("pT_ready")
        bias_ready = sem("bias_ready")
        q_ready = sem("q_ready")
        k_ready = sem("k_ready")
        sT_ready = sem("sT_ready")
        v_ready = sem("v_ready")
        osq_ready = sem("osq_ready")
        osq_summed = sem("osq_summed")
        orms_ready = sem("orms_ready")
        pu_ready = sem("pu_ready")
        pooled_ready = sem("pooled_ready")
        ypool_ready = sem("ypool_ready")
        ga_ready = sem("ga_ready")
        ga_used = sem("ga_used")
        gb_ready = sem("gb_ready")
        gr_ready = sem("gr_ready")
        gated_o = sem("gated_o")
        merged = sem("merged")
        x1_ready = sem("x1_ready")
        sumsq2 = sem("sumsq2")
        xn_ready = sem("xn_ready")
        rms2_ready = sem("rms2_ready")
        h2T_ready = sem("h2T_ready")
        LT_ready = sem("LT_ready")
        top_ready = sem("top_ready")
        exp_ready = sem("exp_ready")
        Mb_ready = sem("Mb_ready")
        part_ready = sem("part_ready")
        resid_ready = sem("resid_ready")
        items_ready = sem("items_ready")

        slot_used = [sem(n) for n in ("glu_half", "glu_done", "lin_half", "lin_done", "down_half", "down_done")]
        glu_done, lin_done, down_done = slot_used[1], slot_used[3], slot_used[5]
        hot_ready = sem("hot_ready")
        gathered = sem("gathered")
        XT_ready = sem("XT_ready")
        bsel_ready = sem("bsel_ready")
        Cg_ready = sem("Cg_ready")
        CT_done = sem("CT_done")
        CT_ready = sem("CT_ready")
        g7_ready = sem("g7_ready")
        sig_ready = sem("sig_ready")
        gs_ready = sem("gs_ready")
        l7_ready = sem("l7_ready")
        act_ready = sem("act_ready")
        aT_done = sem("aT_done")
        aT_ready = sem("aT_ready")
        y_ready = sem("y_ready")
        moe_done = sem("moe_done")
        x2_ready = sem("x2_ready")
        sumsq3 = sem("sumsq3")
        rms3_ready = sem("rms3_ready")
        inv3_ready = sem("inv3_ready")
        pw_done = sem("pw_done")
        pw_ready = sem("pw_ready")
        uT_done = sem("uT_done")
        uT_ready = sem("uT_ready")
        gate_done = sem("gate_done")
        gate_ready = sem("gate_ready")
        x3_ready = sem("x3_ready")
        sumsq4 = sem("sumsq4")
        sumsq4_base = sem("sumsq4_base")
        rms4_ready = sem("rms4_ready")
        out_ready = sem("out_ready")

        def wait_tile_free(pe, n):
            kind, j = TILES[n]
            taken, count = {"q": (q_ready, 2 * j + 2), "k": (k_ready, 2 * j + 2), "v": (v_ready, j + 1),
                            "pool": (pu_ready, j + 1), "ga": (ga_ready, j + 1), "gb": (gb_ready, j + 1),
                            "gr": (gated_o, HEADS + j + 1), "ro": (merged, j + 1), "wo": (x1_ready, j + 1)}[kind]
            pe.wait_ge(taken, count)

        def wait_job_free(pe, n):
            kind, j = JOBS[n]
            taken, count = {"xT": (h32_ready, j + 1), "vec": (vec_ready, 1), "pT": (pT_ready, 1),
                            "scores": (sT_ready, j + 1), "o": (o_copied, j + 1), "ss": (orms_ready, j + 1),
                            "ypool": (ypool_ready, 2 * j + 2), "hT": (h2T_ready, j + 1), "logits": (LT_ready, j + 1),
                            "logitsT": (top_ready, j + 1), "rank": (items_ready, 1)}[kind]
            pe.wait_ge(taken, count)

        def chunk_halves(n, raw):
            if CHUNKS[n][0] == "ro":
                v3 = raw.rearrange("p (k n) -> p k n", k=16)
                return [v3[:, 8 * b:8 * b + 8, :] for b in range(2)]
            v3 = raw.rearrange("p (k n) -> p k n", k=KT)
            return [v3[:, :, 256 * b:256 * b + 256] for b in range(2)]

        def item_loads(n):
            return N1 // 2 if n < 2 else 0

        def even_loaded(i):
            return 16 * (item_loads(0) + 1) + 8 * i

        def input_lo(engine, j):
            t, c = j // 2, j % 2
            to = (slice(None), slice(4 * c, 4 * c + 4), slice(P * t, P * t + P))
            return engine.tensor_tensor(h_lo[to], h32[:, j, :].rearrange("p (k s) -> p k s", k=4),
                                        h_hi[to].bitcast(F32), ALU.subtract)

        block = ctx.enter_context(nc.Block())

        @block.sync
        def _(sp):
            def load_chunk(n):
                kind, j = CHUNKS[n]
                slot = ring[:, n % 2, :]
                if kind in COL:
                    c = COL[kind] + HALF * j
                    src, kts = w_in_v[:, :, c:c + HALF], KT
                elif kind == "ro":
                    src, kts = w_ro_v[:, :, 256 * j:256 * j + 256], 16
                else:
                    src, kts = w_out_v[:, :, HALF * j:HALF * j + HALF], KT
                if n >= 2:
                    sp.wait_ge(lo_ready, 2 * (n - 2) + 2)
                sp.dma_start(slot.rearrange("p (k n) -> p k n", k=kts), src).then_inc(loaded[n % 2], 16)

            def load_item(n, e, odd=0):
                slot, done = (odd_slot[:], loaded_odd) if odd and n == 0 else (ring[:, n, :], loaded[n])
                rows = slice(HALF * (n % 2), HALF * (n % 2) + HALF)
                cols = slice(FF * (n // 2), FF * (n // 2) + FF)
                src = w_gate_up[0, bass.ds(e, 1), rows, cols] if n < 4 else w_down[0, bass.ds(e, 1), rows, :]
                sp.dma_start(slot.rearrange("p (k n) -> p k n", k=4),
                             src.rearrange("a (k p) n -> p (a k) n", p=P)).then_inc(done, 16)

            for t in range(TT):
                sp.dma_start(xs[:, t, :], x_v[:, t, :]).then_inc(x_in[t], 16)
            for n, g in enumerate((g_mix, pool_scale, g_ffn, g_ple)):
                sp.dma_start(vrow[8 * n:8 * n + 8, :], g[0].rearrange("(k p) -> k p", p=P)).then_inc(vec_in, 16)
            load_chunk(0)
            sp.dma_start(rot, c_rot).then_inc(rot_in, 16)
            load_chunk(1)
            sp.dma_start(dec, c_decay).then_inc(dec_in, 16)
            for n in range(2, N1):
                load_chunk(n)
                if CHUNKS[n] == ("ro", 0):
                    sp.wait_ge(pooled_ready, 4)
                    sp.wait_ge(gated_o, HEADS)
                    sp.dma_start(w_ple_sb, w_ple_v).then_inc(w_ple_in, 16)
                if CHUNKS[n] == ("pool", 1):
                    sp.wait_ge(bias_ready, 2)
                    sp.dma_start(wpool, w_pool_v).then_inc(wpool_in, 16)
            for n in range(SLOTS):
                if n < 2:
                    sp.wait_ge(lo_ready, 2 * (N1 - 2 + n) + 2)
                else:
                    sp.wait_ge(tiles_done, chunk_done(N1 - 2 + (n - 2) // 2))
                load_item(n, 0)
            sp.wait_ge(tiles_done, chunk_done(N1 - 1))
            load_item(0, 1, odd=1)
            for n in range(1, SLOTS):
                sp.wait_ge(slot_used[n], 1)
                load_item(n, 1)
            sp.wait_ge(items_ready, 1)
            end = sp.value_load(nitems[0:1, 0:1], min_val=NE, max_val=NE * MAX_BLOCKS)
            with sp.Fori(1, end - 1, 2) as i:
                for odd in range(2):
                    e = sp.snap(sp.to_reg((i + 1 + odd) & (NE - 1)), min_val=0, max_val=NE - 1)
                    sp.wait_ge(slot_used[0], i + odd)
                    load_item(0, e, odd)
                    for n in range(1, SLOTS):
                        sp.wait_ge(slot_used[n], i + 1 + odd)
                        load_item(n, e)
            for n in range(2):
                sp.wait_ge(slot_used[n], end)
                sp.dma_start(ring[:, n, :].rearrange("p (k n) -> p k n", k=KT),
                             w_pg_v[:, :, HALF * n:HALF * n + HALF]).then_inc(loaded[n], 16)
            for n in range(4):
                sp.wait_ge(out_ready, n + 1)
                sp.dma_start(out_v[:, n // 2, HALF * (n % 2):HALF * (n % 2) + HALF],
                             oT[:, 8 + 2 * n:10 + 2 * n, :].rearrange("p c s -> p (c s)")).then_inc(out_done, 16)
            sp.wait_ge(out_done, 16 * 4)

        @block.gpsimd
        def _(pool):
            steps = [0]

            def link(ins):
                steps[0] += 1
                ins.then_inc(pool_step, 1)
                pool.wait_ge(pool_step, steps[0])

            link(nc.gpsimd.memset(ident[:], 0.0))
            nc.gpsimd.affine_select(out=ident[:], in_=ident[:], compare_op=ALU.not_equal, fill=1.0, base=0,
                                    pattern=[[-1, P]], channel_multiplier=1).then_inc(tables, 1)
            nc.gpsimd.memset(eps_t[:], EPS).then_inc(tables, 1)
            nc.gpsimd.memset(ones[:], 1.0).then_inc(tables, 1)
            nc.gpsimd.memset(onesb[:], 1.0).then_inc(tables, 1)
            link(nc.gpsimd.memset(before[:], 1.0))
            nc.gpsimd.affine_select(out=before[:], in_=before[:], compare_op=ALU.is_gt, fill=0.0, base=0,
                                    pattern=[[1, P]], channel_multiplier=-1).then_inc(tables, 1)
            link(nc.gpsimd.memset(pick[:], 0.0))
            for c in range(3):
                nc.gpsimd.affine_select(out=pick[32 * c:32 * c + 32, :], in_=pick[32 * c:32 * c + 32, :],
                                        compare_op=ALU.not_equal, fill=1.0, base=0, pattern=[[-1, NE]],
                                        channel_multiplier=1).then_inc(tables, 1)
                pool.wait_ge(tables, 6 + c)
            nc.gpsimd.iota(slots_io[:], pattern=[[CAP, MAX_BLOCKS + 1], [0, 2], [1, CAP]], base=0,
                           channel_multiplier=0, allow_small_or_imprecise_dtypes=True).then_inc(tables, 1)
            nc.gpsimd.iota(exp_io[:], pattern=[[1, NE]], base=0, channel_multiplier=0,
                           allow_small_or_imprecise_dtypes=True).then_inc(tables, 1)
            nc.gpsimd.iota(steps64[:], pattern=[[CAP, MAX_BLOCKS]], base=0, channel_multiplier=0,
                           allow_small_or_imprecise_dtypes=True).then_inc(tables, 1)

            nc.gpsimd.memset(zero_row[:], 0.0).then_inc(tables, 1)

            for j in (0, 1):
                pool.wait_ge(h_hi_ready, j + 1)
                input_lo(nc.gpsimd, j).then_inc(lo_by_pool, 1)

            def sum_squares(h):
                pool.wait_ge(osq_ready, 2 * h + 2)
                link(nc.gpsimd.tensor_tensor(osq[:, 0], osq[:, 0], osq[:, 1], ALU.add))
                nc.gpsimd.tensor_tensor(osq[:, 0, 0, :], osq[:, 0, 0, :], osq[:, 0, 1, :], ALU.add
                                        ).then_inc(osq_summed, 1)

            pool.wait_ge(jobs_done, job_done("pT"))
            for b in (pu[:, 0], pu[:, 1], pa, pb):
                link(nc.gpsimd.memset(b[:, :, 0:PAD], 0.0))
            pool.wait_ge(count_in, 16)
            pool.wait_ge(bdn_in, 48)
            down_bias = bias_parts[:, 2 * FF:2 * FF + D]
            link(nc.gpsimd.tensor_copy(down_bias, bdn))
            link(nc.gpsimd.tensor_tensor(bdn, bdn, down_bias, ALU.subtract))
            link(nc.gpsimd.tensor_copy(down_bias[32:64, :], bdn[32:64, :]))
            link(nc.gpsimd.tensor_copy(down_bias[64:96, :], bdn[64:96, :]))
            link(nc.gpsimd.tensor_tensor(bdn[64:96, :], bdn[64:96, :], down_bias[64:96, :], ALU.subtract))
            link(nc.gpsimd.tensor_copy(down_bias[64:96, :], bdn[64:96, :]))
            for h in range(HEADS - 1):
                sum_squares(h)
            for g, w in enumerate(WINDOWS):
                if g == 2:
                    sum_squares(HEADS - 1)
                pool.wait_ge(pu_ready, g + 1)
                if g >= 1:
                    pool.wait_ge(pooled_ready, g)
                u = pu[:, g % 2]
                src, shift, n = u, 1, 0
                while shift < w:
                    dst = (pa, pb)[n % 2]
                    link(nc.gpsimd.tensor_tensor(dst[:, :, PAD:], src[:, :, PAD:],
                                                 src[:, :, PAD - shift:PAD + S - shift], ALU.add))
                    src, shift, n = dst, 2 * shift, n + 1
                dst = (pa, pb)[n % 2]
                link(nc.gpsimd.tensor_tensor(dst[:, :, PAD:2 * PAD], src[:, :, PAD:2 * PAD],
                                             recip_count[:, g:g + 1, :].to_broadcast([P, 2, PAD]), ALU.mult))
                link(nc.gpsimd.tensor_scalar(dst[:, :, 2 * PAD:], src[:, :, 2 * PAD:], 1.0 / w, None, ALU.mult))
                nc.gpsimd.tensor_tensor(m[:, 2 * g:2 * g + 2, :], dst[:, :, PAD:], u[:, :, PAD:],
                                        ALU.subtract).then_inc(pooled_ready, 1)
            for j in range(4):
                pool.wait_ge(ypool_ready, 2 * j + 2)
                pool.wait_ge(ga_ready, j + 1)
                nc.gpsimd.tensor_tensor(m[:, 2 * j:2 * j + 2, :], m[:, 2 * j:2 * j + 2, :],
                                        tmp[:, j % 2, :].rearrange("p (a t) -> p a t", a=2),
                                        ALU.mult).then_inc(ga_used, 1)
            for c, t in ((0, 0), (1, 0), (0, 1), (1, 1)):
                pool.wait_ge(part_ready, PART[c, t] + 1)
                if (c, t) == (0, 1):
                    pool.wait_ge(resid_ready, 2)
                elif c == 1:
                    pool.wait_ge(resid_ready, 2 * t + 1)
                nc.gpsimd.tensor_tensor(resid[:, t, :], xn[:, t, :] if c == 0 else resid[:, t, :],
                                        parts[:, c, t, :], ALU.subtract).then_inc(resid_ready, 1)

        @block.scalar
        def _(a):
            steps = [0]

            def link(ins):
                steps[0] += 1
                ins.then_inc(act_step, 1)
                a.wait_ge(act_step, steps[0])

            a.dma_start(recip_count[:], c_count).then_inc(count_in, 16)
            a.dma_start(prow.rearrange("p (t c) s -> p t (c s)", t=TT), p_v).then_inc(p_in, 16)

            def square(src, row, t, done, scratch):
                nc.scalar.activation(scratch, src, ACT.Square, accum_out=stat[:, row, t:t + 1]).then_inc(done, 1)

            def root(row, t, done):
                nc.scalar.activation(stat[:, row + 1, t:t + 1], stat[:, row, t:t + 1], ACT.Sqrt,
                                     bias=eps_t[:, 0:1], scale=1.0 / D).then_inc(done, 1)

            def load_table(func):
                nc.scalar.activation(scrap[:], eps_t[:], func).then_inc(warm, 1)

            a.wait_ge(tables, 2)
            load_table(ACT.Sqrt)
            for t in range(TT):
                a.wait_ge(x_in[t], 16)
                square(xs[:, t, :], 0, t, sumsq, junk)
                a.wait_ge(sumsq, t + 1)
                root(0, t, rms_ready)

            for j in range(4):
                t, c = j // 2, j % 2
                a.wait_ge(h32_ready, j + 1)
                nc.scalar.copy(h_hi[:, 4 * c:4 * c + 4, P * t:P * t + P], h32[:, j, :].rearrange(
                    "p (k s) -> p k s", k=4)).then_inc(h_hi_ready, 1)

            def take_v(h):
                for t in range(TT):
                    a.wait_ge(tiles_done, tile_done("v", 2 * h + t))
                    if h >= 2:
                        a.wait_ge(jobs_done, job_done("o", 2 * (h - 2) + 1))
                    nc.scalar.copy(v[:, h % 2, t, :], tile_bank(TILE["v", 2 * h + t])[:]).then_inc(v_ready, 1)

            def square_o(h):
                for b in range(2):
                    a.wait_ge(jobs_done, job_done("o", 2 * h + b))
                    if h >= 1:
                        a.wait_ge(jobs_done, job_done("ss", h - 1))
                    nc.scalar.activation(osq[:, b, :, :], job_bank("o", 2 * h + b)[:].rearrange(
                        "p (a t) -> p a t", a=2), ACT.Square).then_inc(osq_ready, 1)

            def root_o(h):
                a.wait_ge(jobs_done, job_done("ss", h))
                if h >= 1:
                    a.wait_ge(gated_o, h)
                nc.scalar.activation(rr, job_bank("ss", h)[:, 0:S], ACT.Sqrt, bias=eps_t[:, 0:1],
                                     scale=1.0 / DV).then_inc(orms_ready, 1)

            def split_hi(n):
                a.wait_ge(loaded[n % 2], 16 * (n // 2 + 1))
                if n >= 2:
                    a.wait_ge(tiles_done, chunk_done(n - 2))
                for src, dst in zip(chunk_halves(n, ring[:, n % 2, :]), chunk_halves(n, w_hi[n % 2][:])):
                    nc.scalar.copy(dst, src).then_inc(hi_ready, 1)

            def take_pool(g):
                a.wait_ge(tiles_done, tile_done("pool", g))
                a.wait_ge(pool_step, 7)
                if g >= 2:
                    a.wait_ge(pooled_ready, g - 1)
                nc.scalar.copy(pu[:, g % 2, :, PAD:], tile_bank(TILE["pool", g])[:].rearrange(
                    "p (a t) -> p a t", a=2)).then_inc(pu_ready, 1)

            def scale_ypool(g):
                a.wait_ge(jobs_done, job_done("ypool", g))
                for c in range(2):
                    n = 2 * g + c
                    nc.scalar.activation(m[:, n, :], job_bank("ypool", g)[:, S * c:S * c + S], ACT.Copy,
                                         scale=vec[:, 1, n:n + 1]).then_inc(ypool_ready, 1)

            def gate_a(j):
                a.wait_ge(tiles_done, tile_done("ga", j))
                if j >= 2:
                    a.wait_ge(ga_used, j - 1)
                else:
                    a.wait_ge(gated_o, HEADS + 7 + j)
                nc.scalar.activation(tmp[:, j % 2, :], tile_bank(TILE["ga", j])[:], ACT.Sigmoid
                                     ).then_inc(ga_ready, 1)

            def gate_b(j):
                a.wait_ge(tiles_done, tile_done("gb", j))
                a.wait_ge(jobs_done, job_done("ypool", 3))
                nc.scalar.activation(sigB[:, 2 * j:2 * j + 2, :], tile_bank(TILE["gb", j])[:].rearrange(
                    "p (a t) -> p a t", a=2), ACT.Sigmoid).then_inc(gb_ready, 1)

            def gate_r(j):
                a.wait_ge(tiles_done, tile_done("gr", j))
                if j >= 2:
                    a.wait_ge(gated_o, HEADS + j - 1)
                nc.scalar.activation(tmp[:, j % 2, :], tile_bank(TILE["gr", j])[:], ACT.Sigmoid
                                     ).then_inc(gr_ready, 1)

            split_hi(0)
            for c in range(3):
                a.dma_start(bgu[32 * c:32 * c + 32, :], b_gate_up[0]).then_inc(bgu_in, 16)
                a.dma_start(bdn[32 * c:32 * c + 32, :], b_down[0]).then_inc(bdn_in, 16)
            a.dma_start(wrt[:], w_router[0].rearrange("(k p) e -> p k e", p=P)).then_inc(router_in, 16)
            a.dma_start(brow[:], b_router.to_broadcast([P, NE])).then_inc(router_in, 16)
            for n, (kind, j) in enumerate(CHUNKS):
                if n + 1 < N1:
                    split_hi(n + 1)
                if kind == "v":
                    take_v(j)
                    if j >= 2:
                        root_o(j - 2)
                    if j >= 1:
                        square_o(j - 1)
                elif kind == "pool":
                    take_pool(2 * j)
                    take_pool(2 * j + 1)
                    root_o(2 + j)
                    if j == 0:
                        square_o(3)
                elif kind == "gr":
                    gate_r(2 * j)
                    gate_r(2 * j + 1)
                elif kind == "ga":
                    gate_a(2 * j)
                    gate_a(2 * j + 1)
                    scale_ypool(2 * j)
                    scale_ypool(2 * j + 1)
                elif kind == "gb":
                    gate_b(2 * j)
                    gate_b(2 * j + 1)

            a.wait_ge(merged, 4)
            load_table(ACT.Sqrt)
            a.dma_start(gfin, g_final.rearrange("(a d) -> a d", a=1).to_broadcast([P, D])).then_inc(gfin_in, 16)

            def take_part(c, t):
                if c == 0:
                    a.wait_ge(xn_ready, t + 1)
                else:
                    a.wait_ge(resid_ready, 2 * t + c)
                nc.scalar.copy(parts[:, c, t, :], xn[:, t, :] if c == 0 else resid[:, t, :]).then_inc(part_ready, 1)

            def take_logits(t):
                a.wait_ge(jobs_done, job_done("logits", t))
                nc.scalar.copy(LT[:, P * t:P * t + P], job_bank("logits", t)[0:NE, 0:P]).then_inc(LT_ready, 1)

            def take_pw(n):
                a.wait_ge(pw_done, n + 1)
                a.wait_ge(jobs_done, job_done("logits", 1))
                nc.scalar.copy(pw[:, n // 2, HALF * (n % 2):HALF * (n % 2) + HALF], PW_BANKS[n][:]
                               ).then_inc(pw_ready, 1)

            for t in range(TT):
                a.wait_ge(x1_ready, 3 + t)
                square(xs[:, t, :], 2, t, sumsq2, junk)
                a.wait_ge(sumsq2, t + 1)
                root(2, t, rms2_ready)
                if t == 0:
                    take_part(0, 0)
            take_part(1, 0)
            take_logits(0)
            take_part(0, 1)
            take_logits(1)
            load_table(ACT.Exp)
            take_part(1, 1)
            take_part(2, 0)
            take_pw(0)
            for t in range(TT):
                a.wait_ge(top_ready, t + 1)
                nc.scalar.activation(Eg[:, t, :], L[:, t, :], ACT.Exp, bias=stat[:, 4, t:t + 1]
                                     ).then_inc(exp_ready, 1)
            take_part(2, 1)
            take_pw(1)
            take_pw(2)
            take_pw(3)
            load_table(ACT.Sigmoid)

            a.wait_ge(items_ready, 1)
            end = a.value_load(nitems[0:1, 0:1], min_val=NE, max_val=NE * MAX_BLOCKS)
            with a.Fori(0, end) as i:
                a.wait_ge(g7_ready, i + 1)
                nc.scalar.activation(gs, g7, ACT.Sigmoid, scale=ALPHA).then_inc(sig_ready, 1)
                a.wait_ge(CT_done, i + 1)
                nc.scalar.copy(CT, bank[3][:, 0:S].rearrange("p (t s) -> p t s", t=TT)).then_inc(CT_ready, 1)
                a.wait_ge(aT_done, i + 1)
                nc.scalar.copy(aT, bank[0][:].rearrange("p (j h s) -> p j h s", j=4, h=2)).then_inc(aT_ready, 1)
                a.wait_ge(down_done, i + 1)
                nc.scalar.copy(y, bank[3][:]).then_inc(y_ready, 1)

            load_table(ACT.Sqrt)
            for t in range(TT):
                a.wait_ge(x2_ready, 2 * t + 2)
                square(xs[:, t, :], 5, t, sumsq3, late_junk)
                a.wait_ge(sumsq3, t + 1)
                root(5, t, rms3_ready)
            load_table(ACT.Sigmoid)
            for n in range(4):
                t, h = n // 2, n % 2
                a.wait_ge(gate_done, n + 1)
                a.wait_ge(inv3_ready, t + 1)
                nc.scalar.activation(tmp[:, n % 2, :] if n < 2 else sigB[:, 2 * n - 4:2 * n - 2, :].rearrange(
                    "p a t -> p (a t)"), bank[n][:], ACT.Sigmoid, scale=stat[:, 6, t:t + 1]).then_inc(gate_ready, 1)
                if h == 1:
                    load_table(ACT.Sqrt)
                a.wait_ge(x3_ready, n + 1)
                square(xs[:, t, HALF * h:HALF * h + HALF], 8 + h, t, sumsq4, late_junk[:, 0:HALF])
                if h == 1:
                    a.wait_ge(sumsq4, n + 1)
                    a.wait_ge(sumsq4_base, t + 1)
                    nc.scalar.activation(stat[:, 10, t:t + 1], stat[:, 9, t:t + 1], ACT.Sqrt,
                                         bias=stat[:, 8, t:t + 1], scale=1.0 / D).then_inc(rms4_ready, 1)
                    if t == 0:
                        load_table(ACT.Sigmoid)

        @block.vector
        def _(dve):
            steps = [0]

            def link(ins):
                steps[0] += 1
                ins.then_inc(dve_step, 1)
                dve.wait_ge(dve_step, steps[0])

            def one_hot(e, b):
                for t in range(TT):
                    ins = nc.vector.tensor_scalar(hot[:, t, :], slots_io[:, bass.ds(b, 1), 0, :].rearrange(
                        "p a s -> p (a s)"), pos[:, t, bass.ds(e, 1)], None, ALU.is_equal)
                    ins.then_inc(hot_ready, 1)

            def bias_pick(e):
                nc.vector.tensor_scalar(bsel[0:96, :], ones[0:96, 0:CAP], pick[:, bass.ds(e, 1)], None,
                                        ALU.mult).then_inc(bsel_ready, 1)

            def take_gathered():
                nc.vector.tensor_tensor(XT, bank[2][:].rearrange("p (k s) -> p k s", k=KT),
                                        vec[:, 2, :].unsqueeze(2).to_broadcast([P, KT, CAP]),
                                        ALU.mult).then_inc(XT_ready, 1)

            dve.wait_ge(jobs_done, job_done("vec"))
            nc.vector.tensor_copy(vec[:], job_bank("vec")[:, 0:32].rearrange("p (n k) -> p n k", n=4)
                                  ).then_inc(vec_ready, 1)

            def normalise(row, t, rms, ready):
                dve.wait_ge(rms, t + 1)
                link(nc.vector.reciprocal(stat[:, row, t:t + 1], stat[:, row, t:t + 1]))
                nc.vector.tensor_scalar(xn[:, t, :], xs[:, t, :], stat[:, row, t:t + 1], None,
                                        ALU.mult).then_inc(ready, 1)

            def scaled(out, src, g, c):
                return nc.vector.tensor_tensor(out, src[:].rearrange("p (k s) -> p k s", k=4),
                                               vec[:, g, 4 * c:4 * c + 4].unsqueeze(2).to_broadcast([P, 4, P]),
                                               ALU.mult)

            for t in range(TT):
                normalise(1, t, rms_ready, xs_ready)
            dve.wait_ge(vec_ready, 1)
            for j in range(4):
                dve.wait_ge(jobs_done, job_done("xT", j))
                scaled(h32[:, j, :].rearrange("p (k s) -> p k s", k=4), job_bank("xT", j), 0, j % 2
                       ).then_inc(h32_ready, 1)
            for j in (2, 3):
                dve.wait_ge(h_hi_ready, j + 1)
                input_lo(nc.vector, j).then_inc(hT_ready, 1)

            def split_lo(n):
                for b, (raw, hi, lo) in enumerate(zip(chunk_halves(n, ring[:, n % 2, :]),
                                                      chunk_halves(n, w_hi[n % 2][:]),
                                                      chunk_halves(n, w_lo[n % 2][:]))):
                    dve.wait_ge(hi_ready, 2 * n + b + 1)
                    nc.vector.tensor_tensor(lo, raw, hi.bitcast(F32), ALU.subtract).then_inc(lo_ready, 1)

            def rotate(kind, h, dst, ready):
                n = TILE[kind, h]
                dve.wait_ge(tiles_done, n + 1)
                if h >= 2:
                    dve.wait_ge(jobs_done, job_done("scores", h - 2))
                src = tile_bank(n)[:].rearrange("p (a t) -> p a t", a=2)
                for c in range(2):
                    ins = nc.vector.tensor_tensor(tmp[:, c, :].rearrange("p (a t) -> p a t", a=2), src,
                                                  rot[:, c:c + 1, :].to_broadcast([P, 2, S]), ALU.mult)
                    link(ins)
                nc.vector.tensor_tensor(dst[:, h % 2, 0, :], tmp[:, 0, 0:S], tmp[:, 1, S:2 * S],
                                        ALU.subtract).then_inc(ready, 1)
                nc.vector.tensor_tensor(dst[:, h % 2, 1, :], tmp[:, 0, S:2 * S], tmp[:, 1, 0:S],
                                        ALU.add).then_inc(ready, 1)
                dve.wait_ge(ready, 2 * h + 2)

            def mask_scores(h):
                dve.wait_ge(jobs_done, job_done("scores", h))
                nc.vector.tensor_tensor(sT[:, h, :], job_bank("scores", h)[:, 0:384], dec[:, h, :],
                                        ALU.mult).then_inc(sT_ready, 1)

            def split_biases():
                dve.wait_ge(bgu_in, 48)
                link(nc.vector.tensor_copy(bias_parts[:, 0:2 * FF], bgu))
                link(nc.vector.tensor_tensor(bgu, bgu, bias_parts[:, 0:2 * FF], ALU.subtract))
                nc.vector.tensor_copy(bias_parts[32:64, 0:2 * FF], bgu[32:64, :]).then_inc(bias_ready, 1)
                low = bias_parts[64:96, 0:2 * FF]
                link(nc.vector.tensor_copy(low, bgu[64:96, :]))
                link(nc.vector.tensor_tensor(bgu[64:96, :], bgu[64:96, :], low, ALU.subtract))
                nc.vector.tensor_copy(low, bgu[64:96, :]).then_inc(bias_ready, 1)

            def copy_o(h):
                for b in range(2):
                    dve.wait_ge(osq_ready, 2 * h + b + 1)
                    c = 4 * h + 2 * b
                    nc.vector.tensor_copy(oT[:, c:c + 2, :], job_bank("o", 2 * h + b)[:].rearrange(
                        "p (a t) -> p a t", a=2)).then_inc(o_copied, 1)

            def norm_o(h):
                dve.wait_ge(orms_ready, h + 1)
                link(nc.vector.reciprocal(rr, rr))
                dve.wait_ge(o_copied, 2 * h + 2)
                nc.vector.tensor_tensor(oT[:, 4 * h:4 * h + 4, :], oT[:, 4 * h:4 * h + 4, :],
                                        rr.unsqueeze(1).to_broadcast([P, 4, S]), ALU.mult).then_inc(gated_o, 1)

            def gate_o(j):
                dve.wait_ge(gr_ready, j + 1)
                two = slice(2 * j, 2 * j + 2)
                g = tmp[:, j % 2, :].rearrange("p (a t) -> p a t", a=2)
                link(nc.vector.tensor_tensor(tmp[:, j % 2, :], tile_bank(TILE["gr", j])[:], tmp[:, j % 2, :],
                                             ALU.mult))
                link(nc.vector.tensor_tensor(g, oT[:, two, :], g, ALU.mult))
                link(nc.vector.tensor_copy(o_hi[:, two, :], g))
                nc.vector.tensor_tensor(o_lo[:, two, :], g, o_hi[:, two, :].bitcast(F32),
                                        ALU.subtract).then_inc(gated_o, 1)

            def merge(j):
                dve.wait_ge(tiles_done, tile_done("ro", j))
                two = slice(2 * j, 2 * j + 2)
                link(nc.vector.tensor_tensor(sigB[:, two, :], tile_bank(TILE["ro", j])[:].rearrange(
                    "p (a t) -> p a t", a=2), sigB[:, two, :], ALU.mult))
                link(nc.vector.tensor_tensor(sigB[:, two, :], m[:, two, :], sigB[:, two, :], ALU.add))
                link(nc.vector.tensor_copy(h_hi[:, two, :], sigB[:, two, :]))
                nc.vector.tensor_tensor(h_lo[:, two, :], sigB[:, two, :], h_hi[:, two, :].bitcast(F32),
                                        ALU.subtract).then_inc(merged, 1)

            def add_residual(n):
                dve.wait_ge(tiles_done, tile_done("wo", n))
                cols = slice(HALF * (n // 2), HALF * (n // 2) + HALF)
                nc.vector.tensor_tensor(xs[:, n % 2, cols], xs[:, n % 2, cols], tile_bank(TILE["wo", n])[:],
                                        ALU.add).then_inc(x1_ready, 1)

            split_lo(0)
            for n, (kind, j) in enumerate(CHUNKS):
                if n + 1 < N1:
                    split_lo(n + 1)
                if kind in "qk":
                    if n == 0:
                        dve.wait_ge(rot_in, 16)
                    for h in (2 * j, 2 * j + 1):
                        rotate(kind, h, qr if kind == "q" else kr, q_ready if kind == "q" else k_ready)
                    if (kind, j) == ("q", 1):
                        dve.wait_ge(dec_in, 16)
                        mask_scores(0)
                        mask_scores(1)
                elif kind == "v":
                    if j == 0:
                        mask_scores(2)
                        mask_scores(3)
                        dve.wait_ge(jobs_done, job_done("pT"))
                        nc.vector.tensor_copy(pT, job_bank("pT")[:].rearrange("p (a t) -> p a t", a=2)
                                              ).then_inc(pT_ready, 1)
                        split_biases()
                    if j >= 2:
                        norm_o(j - 2)
                    if j >= 1:
                        copy_o(j - 1)
                elif kind == "pool":
                    norm_o(2 + j)
                    if j == 0:
                        copy_o(3)
                elif kind == "gr":
                    if j == 0:
                        dve.wait_ge(gated_o, HEADS)
                    gate_o(2 * j)
                    gate_o(2 * j + 1)
                elif kind == "ro":
                    if j == 0:
                        dve.wait_ge(gb_ready, 4)
                        dve.wait_ge(ga_used, 4)
                        dve.wait_ge(tables, 11)
                        nc.vector.memset(y, 0.0).then_inc(y_ready, 1)
                        nc.vector.memset(CT, 0.0).then_inc(CT_ready, 1)
                        bias_pick(0)
                    merge(j)
                elif kind == "wo":
                    if j == 0:
                        add_residual(0)
                        add_residual(1)

            def take_hT(j):
                dve.wait_ge(jobs_done, job_done("hT", j))
                t, c = j // 2, j % 2
                scaled(h2T[:, 4 * c:4 * c + 4, P * t:P * t + P], job_bank("hT", j), 2, c).then_inc(h2T_ready, 1)

            add_residual(2)
            normalise(3, 0, rms2_ready, xn_ready)
            add_residual(3)
            take_hT(0)
            take_hT(1)
            normalise(3, 1, rms2_ready, xn_ready)
            take_hT(2)
            take_hT(3)

            dve.wait_ge(router_in, 32)
            for t in range(TT):
                dve.wait_ge(jobs_done, job_done("logitsT", t))
                link(nc.vector.scalar_tensor_tensor(out=L[:, t, :], in0=job_bank("logitsT", t)[:, 0:NE],
                                                    scalar=stat[:, 3, t:t + 1], in1=brow[:],
                                                    op0=ALU.mult, op1=ALU.add))
                link(nc.vector.max(top[:, t, :], L[:, t, :]))
                nc.vector.tensor_scalar(stat[:, 4, t:t + 1], top[:, t, 0:1], -1.0, None,
                                        ALU.mult).then_inc(top_ready, 1)
                link(nc.vector.max_index(topi[:, t, :], top[:, t, :], L[:, t, :]))
                link(nc.vector.tensor_copy(topf[:, t, :], topi[:, t, :]))
                link(nc.vector.tensor_scalar(Msel[:, t, :], exp_io[:], topf[:, t, 0:1], None, ALU.is_equal))
                for k in range(1, TOPK):
                    link(nc.vector.scalar_tensor_tensor(out=Msel[:, t, :], in0=exp_io[:],
                                                        scalar=topf[:, t, k:k + 1], in1=Msel[:, t, :],
                                                        op0=ALU.is_equal, op1=ALU.add))
                nc.vector.tensor_copy(Mb[:, t, :], Msel[:, t, :]).then_inc(Mb_ready, 1)
            dve.wait_ge(jobs_done, job_done("rank"))
            rank = job_bank("rank")[:, 0:2 * NE].rearrange("p (t e) -> p t e", t=TT)
            link(nc.vector.scalar_tensor_tensor(out=pos[:], in0=rank, scalar=1.0, in1=Msel[:],
                                                op0=ALU.add, op1=ALU.mult))
            link(nc.vector.tensor_scalar(pos[:], pos[:], -1.0, None, ALU.add))
            one_hot(0, 0)
            link(nc.vector.reduce_max(nit[:, 0:1], job_bank("rank")[0:1, 2 * NE:3 * NE], AX_X))
            link(nc.vector.tensor_scalar(nit[:, 2:2 + MAX_BLOCKS], steps64[:], nit[:, 0:1], float(NE),
                                         ALU.is_lt, ALU.mult))
            link(nc.vector.reduce_sum(nit[:, 1:2], nit[:, 2:2 + MAX_BLOCKS], AX_X))
            nc.vector.tensor_copy(nitems[:], nit[:, 1:2]).then_inc(items_ready, 1)
            dve.wait_ge(gathered, 1)
            take_gathered()
            dve.wait_ge(exp_ready, TT)
            link(nc.vector.tensor_tensor(Eg[:], Eg[:], Msel[:], ALU.mult))
            link(nc.vector.reduce_sum(stat[:, 7, :], Eg[:], AX_X))
            link(nc.vector.reciprocal(stat[:, 7, :], stat[:, 7, :]))
            for t in range(TT):
                link(nc.vector.tensor_scalar(G[:, t, :], Eg[:, t, :], stat[:, 7, t:t + 1], None, ALU.mult))

            dve.wait_ge(items_ready, 1)
            end = dve.value_load(nitems[0:1, 0:1], min_val=NE, max_val=NE * MAX_BLOCKS)
            with dve.Fori(0, end) as i:
                e, b = i & (NE - 1), i >> 5
                nxt = i + 1
                dve.wait_ge(CT_done, i)
                for t in range(TT):
                    nc.vector.tensor_scalar(Cg[:, t, :], slots_io[:, bass.ds(b, 1), :, :].rearrange(
                        "p a h s -> p (a h s)"), pos[:, t, bass.ds(e, 1)], G[:, t, bass.ds(e, 1)],
                        ALU.is_equal, ALU.mult).then_inc(Cg_ready, 1)
                dve.wait_ge(gathered, i + 1)
                one_hot(nxt & (NE - 1), nxt >> 5)
                dve.wait_ge(glu_done, i + 1)
                nc.vector.tensor_scalar(g7, bank[0][:], LIMIT, None, ALU.min).then_inc(g7_ready, 1)
                dve.wait_ge(sig_ready, i + 1)
                nc.vector.tensor_tensor(gs, g7, gs, ALU.mult).then_inc(gs_ready, 1)
                dve.wait_ge(lin_done, i + 1)
                nc.vector.tensor_scalar(l7, bank[1][:], LIMIT, -LIMIT, ALU.min, ALU.max).then_inc(l7_ready, 1)
                dve.wait_ge(gs_ready, i + 1)
                dve.wait_ge(l7_ready, i + 1)
                nc.vector.scalar_tensor_tensor(out=act, in0=l7, scalar=1.0, in1=gs, op0=ALU.add,
                                               op1=ALU.mult).then_inc(act_ready, 1)
                dve.wait_ge(gathered, i + 2)
                take_gathered()
                dve.wait_ge(slot_used[4], i + 1)
                bias_pick(nxt & (NE - 1))

            for n in range(4):
                dve.wait_ge(moe_done, n + 1)
                cols = slice(HALF * (n % 2), HALF * (n % 2) + HALF)
                nc.vector.tensor_tensor(xs[:, n // 2, cols], xs[:, n // 2, cols], bank[4 + n][:],
                                        ALU.add).then_inc(x2_ready, 1)
            for n in range(4):
                t, c = n // 2, n % 2
                dve.wait_ge(uT_done, n + 1)
                scaled(uT[:, 4 * c:4 * c + 4, P * t:P * t + P], bank[4 + n], 3, c).then_inc(uT_ready, 1)
            for t in range(TT):
                dve.wait_ge(rms3_ready, t + 1)
                nc.vector.reciprocal(stat[:, 6, t:t + 1], stat[:, 6, t:t + 1]).then_inc(inv3_ready, 1)
            dve.wait_ge(pw_ready, 4)
            dve.wait_ge(gfin_in, 16)
            for n in range(4):
                t, h = n // 2, n % 2
                cols = slice(HALF * h, HALF * h + HALF)
                dve.wait_ge(gate_ready, n + 1)
                src = tmp[:, n % 2, :] if n < 2 else sigB[:, 2 * n - 4:2 * n - 2, :].rearrange("p a t -> p (a t)")
                link(nc.vector.tensor_tensor(pw[:, t, cols], pw[:, t, cols], src, ALU.mult))
                nc.vector.tensor_tensor(xs[:, t, cols], xs[:, t, cols], pw[:, t, cols],
                                        ALU.add).then_inc(x3_ready, 1)
                if h == 0:
                    dve.wait_ge(sumsq4, n + 1)
                    nc.vector.tensor_scalar(stat[:, 8, t:t + 1], stat[:, 8, t:t + 1], 1.0 / D, EPS,
                                            ALU.mult, ALU.add).then_inc(sumsq4_base, 1)
                else:
                    dve.wait_ge(x3_ready, n + 1)
                    dve.wait_ge(rms4_ready, t + 1)
                    link(nc.vector.reciprocal(stat[:, 10, t:t + 1], stat[:, 10, t:t + 1]))
                    for c in range(2):
                        half = slice(HALF * c, HALF * c + HALF)
                        at = 8 + 4 * t + 2 * c
                        nc.vector.scalar_tensor_tensor(out=oT[:, at:at + 2, :].rearrange("p c s -> p (c s)"),
                                                       in0=xs[:, t, half], scalar=stat[:, 10, t:t + 1],
                                                       in1=gfin[:, half], op0=ALU.mult,
                                                       op1=ALU.mult).then_inc(out_ready, 1)

        @block.tensor
        def _(pe):
            def take_job(kind, j=0):
                n = JOB[kind, j]
                if n >= 4:
                    wait_job_free(pe, n - 4)
                return bank[4 + n % 4]

            def transposes(kind, t, src):
                for c in range(2):
                    dst = take_job(kind, 2 * t + c)
                    for k in range(4):
                        col = P * (4 * c + k)
                        last = nc.tensor.transpose(dst[:, P * k:P * k + P], src[:, t, col:col + P], ident[:])
                    last.then_inc(jobs_done, 1)

            pe.wait_ge(tables, 4)
            pe.wait_ge(vec_in, 64)
            nc.tensor.transpose(take_job("vec")[:, 0:32], vrow[:], ident[0:32, 0:32]).then_inc(jobs_done, 1)
            for t in range(TT):
                pe.wait_ge(xs_ready, t + 1)
                transposes("xT", t, xn)

            def transpose_embeddings():
                pe.wait_ge(p_in, 16)
                dst = take_job("pT")
                pr = prow.rearrange("p (t c) s -> p t (c s)", t=TT)
                for c in range(2):
                    for t in range(TT):
                        last = nc.tensor.transpose(dst[:, S * c + P * t:S * c + P * t + P],
                                                   pr[:, t, P * c:P * c + P], ident[:])
                last.then_inc(jobs_done, 1)

            def product(dst, stationary, moving, k, kts):
                (s_hi, s_lo), (m_hi, m_lo) = stationary, moving
                nc.tensor.matmul(dst, s_hi, m_hi, start=(k == 0), stop=False)
                nc.tensor.matmul(dst, s_hi, m_lo, start=False, stop=False)
                return nc.tensor.matmul(dst, s_lo, m_hi, start=False, stop=(k == kts - 1))

            def chunk(n):
                kind, j = CHUNKS[n]
                kts = 16 if kind == "ro" else KT
                w = [x[n % 2][:].rearrange("p (k n) -> p k n", k=kts) for x in (w_hi, w_lo)]
                src = (o_hi, o_lo) if kind == "ro" else (h_hi, h_lo)
                for b in range(1 if kind == "ro" else 2):
                    t = TILE[kind, j if kind == "ro" else 2 * j + b]
                    pe.wait_ge(lo_ready, 2 * n + 2 if kind in ("v", "ro", "wo") else 2 * n + b + 1)
                    if t >= 4:
                        wait_tile_free(pe, t - 4)
                    dst = tile_bank(t)
                    if kind in ("v", "wo"):
                        for k in range(kts):
                            if kind == "wo" and k % 2 == 0:
                                pe.wait_ge(merged, k // 2 + 1)
                            last = product(dst[:], [x[:, k, P * b:P * b + P] for x in src],
                                           [x[:, k, :] for x in w], k, kts)
                    else:
                        for c in range(2):
                            col = P * (2 * b + c)
                            for k in range(kts):
                                last = product(dst[:, S * c:S * c + S], [x[:, k, col:col + P] for x in w],
                                               [x[:, k, :] for x in src], k, kts)
                    last.then_inc(tiles_done, 1)

            def scores(h):
                pe.wait_ge(q_ready, 2 * h + 2)
                pe.wait_ge(k_ready, 2 * h + 2)
                dst = take_job("scores", h)
                for a in range(2):
                    nc.tensor.matmul(dst[:, 0:S], kr[:, h % 2, a, 0:P], qr[:, h % 2, a, :],
                                     start=(a == 0), stop=(a == 1))
                for a in range(2):
                    last = nc.tensor.matmul(dst[:, S:S + P], kr[:, h % 2, a, P:S], qr[:, h % 2, a, P:S],
                                            start=(a == 0), stop=(a == 1))
                last.then_inc(jobs_done, 1)

            def outputs(h):
                pe.wait_ge(sT_ready, h + 1)
                pe.wait_ge(v_ready, 2 * h + 2)
                for b in range(2):
                    dst = take_job("o", 2 * h + b)
                    for c in range(2):
                        col = P * (2 * b + c)
                        nc.tensor.matmul(dst[:, S * c:S * c + S], v[:, h % 2, 0, col:col + P], sT[:, h, 0:S],
                                         start=True, stop=False)
                        last = nc.tensor.matmul(dst[:, S * c + P:S * c + S], v[:, h % 2, 1, col:col + P],
                                                sT[:, h, S:S + P], start=False, stop=True)
                    last.then_inc(jobs_done, 1)

            def sum_squares(h):
                pe.wait_ge(osq_summed, h + 1)
                nc.tensor.matmul(take_job("ss", h)[:, 0:S], ones[:], osq[:, 0, 0, :], start=True, stop=True
                                 ).then_inc(jobs_done, 1)

            def pool_project(g):
                pe.wait_ge(pooled_ready, g + 1)
                pe.wait_ge(wpool_in, 16)
                dst = take_job("ypool", g)
                for c in range(2):
                    for k in range(2):
                        last = nc.tensor.matmul(dst[:, S * c:S * c + S], wpool[:, g, k, P * c:P * c + P],
                                                m[:, 2 * g + k, :], start=(k == 0), stop=(k == 1))
                last.then_inc(jobs_done, 1)

            pe.wait_ge(lo_by_pool, 2)
            pe.wait_ge(hT_ready, 2)
            for n, (kind, j) in enumerate(CHUNKS):
                if (kind, j) == ("ro", 0):
                    pe.wait_ge(gated_o, HEADS + 8)
                chunk(n)
                if (kind, j) == ("q", 1):
                    scores(0)
                    scores(1)
                elif (kind, j) == ("v", 0):
                    scores(2)
                    scores(3)
                    transpose_embeddings()
                elif kind == "v":
                    if j >= 2:
                        sum_squares(j - 2)
                    outputs(j - 1)
                elif kind == "pool":
                    sum_squares(2 + j)
                    if j == 0:
                        outputs(3)
                elif kind == "ga":
                    pool_project(2 * j)
                    pool_project(2 * j + 1)

            def embed(n):
                t, h = n // 2, n % 2
                for k in range(2):
                    last = nc.tensor.matmul(PW_BANKS[n][:], pT[:, k, P * t:P * t + P],
                                            w_ple_sb[:, k, HALF * h:HALF * h + HALF], start=(k == 0), stop=(k == 1))
                last.then_inc(pw_done, 1)

            def logits(t):
                dst = take_job("logits", t)
                for k in range(KT):
                    if k % 4 == 0:
                        pe.wait_ge(h2T_ready, 2 * t + k // 4 + 1)
                    last = nc.tensor.matmul(dst[0:NE, 0:P], wrt[:, k, :], h2T[:, k, P * t:P * t + P],
                                            start=(k == 0), stop=(k == KT - 1))
                last.then_inc(jobs_done, 1)

            for t in range(TT):
                pe.wait_ge(x1_ready, 3 + t)
                transposes("hT", t, xs)
            pe.wait_ge(router_in, 32)
            pe.wait_ge(w_ple_in, 16)
            pe.wait_ge(pT_ready, 1)
            logits(0)
            logits(1)
            for t in range(TT):
                pe.wait_ge(LT_ready, t + 1)
                nc.tensor.transpose(take_job("logitsT", t)[:, 0:NE], LT[:, P * t:P * t + P],
                                    ident[0:NE, 0:NE]).then_inc(jobs_done, 1)
            embed(0)
            embed(1)
            pe.wait_ge(Mb_ready, TT)
            pe.wait_ge(tables, 12)
            dst = take_job("rank")
            for n, terms in enumerate((((before, 0),), ((onesb, 0), (before, 1)), ((onesb, 0), (onesb, 1)))):
                for k, (mat, t) in enumerate(terms):
                    last = nc.tensor.matmul(dst[:, NE * n:NE * n + NE], mat[:], Mb[:, t, :],
                                            start=(k == 0), stop=(k == len(terms) - 1))
            last.then_inc(jobs_done, 1)
            embed(2)
            embed(3)

            def gather():
                for k in range(KT):
                    for c in range(3):
                        for t in range(TT):
                            last = nc.tensor.matmul(bank[2][:, CAP * k:CAP * k + CAP],
                                                    parts[:, c, t, P * k:P * k + P], hot[:, t, :],
                                                    start=(c == 0 and t == 0), stop=(c == 2 and t == TT - 1))
                last.then_inc(gathered, 1)

            def combine(final):
                for t in range(TT):
                    for h in range(2):
                        last = nc.tensor.matmul(bank[4 + 2 * t + h][:], CT[CAP * h:CAP * h + CAP, t, :],
                                                y[CAP * h:CAP * h + CAP, :], start=False, stop=final,
                                                skip_group_check=True)
                        if final:
                            last.then_inc(moe_done, 1)

            pe.wait_ge(part_ready, len(PARTS))
            pe.wait_ge(hot_ready, TT)
            pe.wait_ge(pw_ready, 1)
            gather()
            pe.wait_ge(items_ready, 1)
            for n in range(4):
                nc.tensor.matmul(bank[4 + n][:], zero_row[:, 0:P], zero_row[:], start=True, stop=False,
                                 skip_group_check=True)
            pe.wait_ge(pw_ready, 4)
            pe.wait_ge(bias_ready, 2)
            end = pe.value_load(nitems[0:1, 0:1], min_val=NE, max_val=NE * MAX_BLOCKS)
            def item(i, odd):
                def up(first, dst):
                    for h in range(2):
                        nc.tensor.matmul(dst[CAP * h:CAP * h + CAP, :], bsel[0:96, :],
                                         bias_parts[:, FF * (first // 2) + HALF * h:FF * (first // 2) + HALF * (h + 1)],
                                         start=True, stop=False)
                    for c in range(2):
                        n = first + c
                        w = (odd_slot[:] if odd and n == 0 else ring[:, n, :]).rearrange("p (k n) -> p k n", k=4)
                        if n > 0:
                            pe.wait_ge(loaded[n], 16 * (item_loads(n) + 1) + 16 * i)
                        elif odd:
                            pe.wait_ge(loaded_odd, 8 * i + 8)
                        else:
                            pe.wait_ge(loaded[0], even_loaded(i))
                        for k in range(4):
                            for h in range(2):
                                last = nc.tensor.matmul(dst[CAP * h:CAP * h + CAP, :], XT[:, 4 * c + k, :],
                                                        w[:, k, HALF * h:HALF * h + HALF],
                                                        start=False, stop=(c == 1 and k == 3))
                        last.then_inc(slot_used[n], 1)

                pe.wait_ge(XT_ready, i + 1)
                pe.wait_ge(bsel_ready, i + 1)
                up(0, bank[0])
                pe.wait_ge(y_ready, i + 1)
                pe.wait_ge(CT_ready, i + 1)
                combine(False)
                up(2, bank[1])
                pe.wait_ge(Cg_ready, 2 * i + 2)
                for t in range(TT):
                    last = nc.tensor.transpose(bank[3][:, P * t:P * t + P], Cg[:, t, :], ident[:])
                last.then_inc(CT_done, 1)
                pe.wait_ge(hot_ready, 2 * i + 4)
                gather()
                pe.wait_ge(act_ready, i + 1)
                for j in range(4):
                    last = nc.tensor.transpose(bank[0][:, P * j:P * j + P], act[:, P * j:P * j + P], ident[:])
                last.then_inc(aT_done, 1)
                pe.wait_ge(aT_ready, i + 1)
                pe.wait_ge(CT_ready, i + 2)
                for h in range(2):
                    nc.tensor.matmul(bank[3][CAP * h:CAP * h + CAP, :], bsel[0:96, :],
                                     bias_parts[:, 2 * FF + HALF * h:2 * FF + HALF * (h + 1)],
                                     start=True, stop=False)
                for c in range(2):
                    n = 4 + c
                    w = ring[:, n, :].rearrange("p (k n) -> p k n", k=4)
                    pe.wait_ge(loaded[n], 16 * (item_loads(n) + 1) + 16 * i)
                    for k in range(4):
                        for h in range(2):
                            last = nc.tensor.matmul(bank[3][CAP * h:CAP * h + CAP, :], aT[:, k, c, :],
                                                    w[:, k, HALF * h:HALF * h + HALF],
                                                    start=False, stop=(c == 1 and k == 3))
                    last.then_inc(slot_used[n], 1)
            with pe.Fori(0, end, 2) as i:
                item(i, 0)
                item(i + 1, 1)
            pe.wait_ge(y_ready, end + 1)
            combine(True)

            for n in range(4):
                t, c = n // 2, n % 2
                pe.wait_ge(x2_ready, n + 1)
                for k in range(4):
                    col = P * (4 * c + k)
                    last = nc.tensor.transpose(bank[4 + n][:, P * k:P * k + P], xs[:, t, col:col + P], ident[:])
                last.then_inc(uT_done, 1)
            for n in range(4):
                t, h = n // 2, n % 2
                pe.wait_ge(uT_ready, 2 * t + 2)
                pe.wait_ge(loaded[h], even_loaded(end) if h == 0 else 16 * (item_loads(h) + 1) + 16 * end)
                w = ring[:, h, :].rearrange("p (k n) -> p k n", k=KT)
                for k in range(KT):
                    last = nc.tensor.matmul(bank[n][:], uT[:, k, P * t:P * t + P], w[:, k, :],
                                            start=(k == 0), stop=(k == KT - 1))
                last.then_inc(gate_done, 1)


def constants():
    half = D // HEADS // 2
    inv = np.power(np.float32(10000.0), -np.linspace(0.0, 1.0, half, dtype=np.float32)).astype(np.float32)
    ang = (inv[:, None] * np.arange(S, dtype=np.float32)[None, :]).astype(np.float64)
    rot = np.stack([np.cos(ang), np.sin(ang)], axis=1).astype(np.float32)
    tok = np.arange(S)
    gap = np.abs(tok[:, None] - tok[None, :])
    seen = tok[:, None] // CHUNK <= tok[None, :] // CHUNK
    decay = np.empty((P, HEADS, S + P), np.float32)
    for h in range(HEADS):
        full = np.where(seen, np.exp(np.log(1.0 - 2.0 ** (-5.0 - h)) * gap), 0.0) * (D // HEADS) ** -0.5
        decay[:, h, :S] = full[:P]
        decay[:, h, S:] = full[P:, P:]
    count = np.stack([1.0 / np.minimum(tok[:PAD] + 1.0, w) for w in WINDOWS]).astype(np.float32)
    return {"c_rot": rot, "c_decay": decay, "c_count": np.ascontiguousarray(np.broadcast_to(count, (P, 4, PAD)))}


_INS = ["x", "p", "g_mix", "w_in", "w_pool", "pool_scale", "w_ret_o", "w_out", "g_ffn", "w_router", "b_router",
        "w_gate_up", "b_gate_up", "w_down", "b_down", "g_ple", "w_ple_gate", "w_ple", "g_final"]


def kernel(**inputs):
    import concourse.bacc as bacc
    from concourse.bass_utils import run_bass_kernel_spmd

    nc = bacc.Bacc("TRN2", target_bir_lowering=False, num_devices=1)
    arrays, args = {}, []
    values = {name: np.ascontiguousarray(inputs[name]) for name in _INS} | constants()
    for name, a in values.items():
        arrays[f"in_{name}_dram"] = a
        args.append(nc.dram_tensor(f"in_{name}_dram", a.shape, mybir.dt.from_np(a.dtype), kind="ExternalInput").ap())
    args.append(nc.dram_tensor("out_dram", (1, S, D), F32, kind="ExternalOutput").ap())
    build_kernel(nc, *args)
    r = run_bass_kernel_spmd(nc, [arrays], core_ids=[0])
    return r.results[0]["out_dram"]
```
